# Optimizing a Trainium2 kernel written in Bass

```python
import jax, jax.numpy as jnp
from jax import lax
import numpy as np

D_MODEL = 1024
BATCH = 1
SEQ = 512
DEPTH = 2
DEC_BATCH = 1
DEC_SEQ = 256
PAST_LEN = 128

N_META = 16
BLOCK = 128
WINDOW = 128
N_HEADS = 8
N_KV_HEADS = 2
GQA_GROUP = N_HEADS // N_KV_HEADS
HEAD_DIM = 64
Q_DIM = N_HEADS * HEAD_DIM
KV_DIM = N_KV_HEADS * HEAD_DIM
POOL_DIM = D_MODEL // 2
POOL_WINDOWS = (2, 4, 8, 16)
N_POOL_GROUPS = len(POOL_WINDOWS)
POOL_GROUP = POOL_DIM // N_POOL_GROUPS
IN_DIM = Q_DIM + 2 * KV_DIM + POOL_DIM
MIX_DIM = Q_DIM + POOL_DIM
N_FOURIER_GROUPS = 4
FOURIER_GROUP = D_MODEL // N_FOURIER_GROUPS
D_FF = 2816
N_EVEN = (DEPTH + 1) // 2
N_ODD = DEPTH // 2
EPS = 1e-6
NEG_INF = -1e30

kernel_name = "hybrid_bidir_swa_pool_fnet_encoder"

def rms_norm(x, g):
    xf = x.astype(jnp.float32)
    y = xf * lax.rsqrt(jnp.mean(xf * xf, axis=-1, keepdims=True) + EPS)
    return (y * g.astype(jnp.float32)).astype(x.dtype)

def swiglu(x, w_gate, w_up, w_down):
    return (jax.nn.silu(x @ w_gate) * (x @ w_up)) @ w_down

def alibi_slopes():
    h = jnp.arange(1, N_HEADS + 1, dtype=jnp.float32)
    return jnp.exp2(-8.0 * h / N_HEADS)

def window_attention(q, k, v, sink):
    B, L = q.shape[:2]
    pad_front = BLOCK - N_META
    Lp = L + pad_front
    nb = Lp // BLOCK
    qp = jnp.pad(q, ((0, 0), (pad_front, 0), (0, 0), (0, 0)))
    qp = qp.reshape(B, nb, BLOCK, N_KV_HEADS, GQA_GROUP, HEAD_DIM)

    def kv_windows(a):
        ap = jnp.pad(a, ((0, 0), (pad_front + BLOCK, BLOCK), (0, 0), (0, 0)))
        ap = ap.reshape(B, nb + 2, BLOCK, N_KV_HEADS, HEAD_DIM)
        return jnp.concatenate([ap[:, :-2], ap[:, 1:-1], ap[:, 2:]], axis=2)

    kw = kv_windows(k)
    vw = kv_windows(v)
    scale = HEAD_DIM ** -0.5
    s = jnp.einsum('bnqkgd,bnskd->bnkgqs', qp, kw).astype(jnp.float32) * scale

    qpos = jnp.arange(nb)[:, None] * BLOCK + jnp.arange(BLOCK)[None, :]
    kpos = (jnp.arange(nb)[:, None] - 1) * BLOCK + jnp.arange(3 * BLOCK)[None, :]
    dist = jnp.abs(qpos[:, :, None] - kpos[:, None, :])
    valid = (dist <= WINDOW) & (kpos[:, None, :] >= pad_front) & (kpos[:, None, :] < Lp)
    slopes = alibi_slopes().reshape(N_KV_HEADS, GQA_GROUP)
    bias = -slopes[None, :, :, None, None] * dist[:, None, None].astype(jnp.float32)
    s = jnp.where(valid[:, None, None], s + bias[None], NEG_INF)

    sk = sink.astype(jnp.float32).reshape(N_KV_HEADS, GQA_GROUP)[None, None, :, :, None]
    m = jnp.maximum(jnp.max(s, axis=-1), sk)
    p = jnp.exp(s - m[..., None])
    denom = jnp.sum(p, axis=-1) + jnp.exp(sk - m)
    o = jnp.einsum('bnkgqs,bnskd->bnkgqd', p.astype(v.dtype), vw).astype(jnp.float32)
    o = (o / denom[..., None]).astype(q.dtype)
    o = o.transpose(0, 1, 4, 2, 3, 5).reshape(B, Lp, Q_DIM)
    return o[:, pad_front:]

def multiscale_pool(u, w_pool, pool_scale):
    B, L, _ = u.shape
    uf = u.astype(jnp.float32).reshape(B, L, N_POOL_GROUPS, POOL_GROUP)
    c = jnp.concatenate([jnp.zeros((B, 1, N_POOL_GROUPS, POOL_GROUP), jnp.float32),
                         jnp.cumsum(uf, axis=1)], axis=1)
    t = jnp.arange(L)
    outs = []
    for g, w in enumerate(POOL_WINDOWS):
        lo = jnp.clip(t - w // 2, 0, L)
        hi = jnp.clip(t + w - w // 2, 0, L)
        cnt = (hi - lo).astype(jnp.float32)[None, :, None]
        outs.append((c[:, hi, g] - c[:, lo, g]) / cnt)
    pooled = (jnp.stack(outs, axis=2) - uf).astype(u.dtype)
    y = jnp.einsum('blgc,gcd->blgd', pooled, w_pool).reshape(B, L, POOL_DIM)
    return y * pool_scale

def even_mixer(h, w_in, sink, w_pool, pool_scale, w_out):
    B, L, _ = h.shape
    z = h @ w_in
    q, k, v, u = jnp.split(z, [Q_DIM, Q_DIM + KV_DIM, Q_DIM + 2 * KV_DIM], axis=-1)
    q = q.reshape(B, L, N_HEADS, HEAD_DIM)
    k = k.reshape(B, L, N_KV_HEADS, HEAD_DIM)
    v = v.reshape(B, L, N_KV_HEADS, HEAD_DIM)
    a = window_attention(q, k, v, sink)
    p = multiscale_pool(u, w_pool, pool_scale)
    return jnp.concatenate([a, p], axis=-1) @ w_out

def fourier_mixer(h, w_out):
    B, L, _ = h.shape
    hf = h.astype(jnp.float32).reshape(B, L, N_FOURIER_GROUPS, FOURIER_GROUP)
    f = jnp.fft.fft2(hf, axes=(1, 3), norm='ortho').real.astype(h.dtype).reshape(B, L, D_MODEL)
    return f @ w_out

def trunk(x, meta_tokens, norm_ffn1, ffn1_w_gate, ffn1_w_up, ffn1_w_down, norm_mix,
          w_in_ap, attn_sink, pool_w, pool_scale, w_out_ap, w_out_fourier,
          norm_ffn2, ffn2_w_gate, ffn2_w_up, ffn2_w_down, norm_final):
    B = x.shape[0]
    meta = jnp.broadcast_to(meta_tokens[None].astype(x.dtype), (B, N_META, D_MODEL))
    h = jnp.concatenate([meta, x], axis=1)
    for layer in range(DEPTH):
        h = h + 0.5 * swiglu(rms_norm(h, norm_ffn1[layer]), ffn1_w_gate[layer],
                             ffn1_w_up[layer], ffn1_w_down[layer])
        hn = rms_norm(h, norm_mix[layer])
        if layer % 2 == 0:
            i = layer // 2
            h = h + even_mixer(hn, w_in_ap[i], attn_sink[i], pool_w[i], pool_scale[i], w_out_ap[i])
        else:
            h = h + fourier_mixer(hn, w_out_fourier[layer // 2])
        h = h + 0.5 * swiglu(rms_norm(h, norm_ffn2[layer]), ffn2_w_gate[layer],
                             ffn2_w_up[layer], ffn2_w_down[layer])
    return rms_norm(h, norm_final)[:, N_META:]

def setup_inputs(seed: int = 0) -> dict:
    key = jax.random.key(seed)
    ks = jax.random.split(key, 20)
    f32 = jnp.float32

    def nrm(k, shape, scale):
        return jax.random.normal(k, shape, f32) * scale

    def gain(k, shape):
        return 1.0 + 0.02 * jax.random.normal(k, shape, f32)

    return {
        "x_prompt": nrm(ks[0], (BATCH, SEQ, D_MODEL), 1.0),
        "x_sample": nrm(ks[1], (DEC_BATCH, DEC_SEQ, D_MODEL), 1.0),
        "meta_tokens": nrm(ks[2], (N_META, D_MODEL), 1.0),
        "norm_ffn1": gain(ks[3], (DEPTH, D_MODEL)),
        "ffn1_w_gate": nrm(ks[4], (DEPTH, D_MODEL, D_FF), D_MODEL ** -0.5),
        "ffn1_w_up": nrm(ks[5], (DEPTH, D_MODEL, D_FF), D_MODEL ** -0.5),
        "ffn1_w_down": nrm(ks[6], (DEPTH, D_FF, D_MODEL), D_FF ** -0.5),
        "norm_mix": gain(ks[7], (DEPTH, D_MODEL)),
        "w_in_ap": nrm(ks[8], (N_EVEN, D_MODEL, IN_DIM), D_MODEL ** -0.5),
        "attn_sink": nrm(ks[9], (N_EVEN, N_HEADS), 0.5),
        "pool_w": nrm(ks[10], (N_EVEN, N_POOL_GROUPS, POOL_GROUP, POOL_GROUP), POOL_GROUP ** -0.5),
        "pool_scale": gain(ks[11], (N_EVEN, POOL_DIM)),
        "w_out_ap": nrm(ks[12], (N_EVEN, MIX_DIM, D_MODEL), MIX_DIM ** -0.5),
        "w_out_fourier": nrm(ks[13], (N_ODD, D_MODEL, D_MODEL), D_MODEL ** -0.5),
        "norm_ffn2": gain(ks[14], (DEPTH, D_MODEL)),
        "ffn2_w_gate": nrm(ks[15], (DEPTH, D_MODEL, D_FF), D_MODEL ** -0.5),
        "ffn2_w_up": nrm(ks[16], (DEPTH, D_MODEL, D_FF), D_MODEL ** -0.5),
        "ffn2_w_down": nrm(ks[17], (DEPTH, D_FF, D_MODEL), D_FF ** -0.5),
        "norm_final": gain(ks[18], (D_MODEL,)),
    }

def reference(x_prompt, x_sample, meta_tokens, norm_ffn1, ffn1_w_gate, ffn1_w_up, ffn1_w_down,
              norm_mix, w_in_ap, attn_sink, pool_w, pool_scale, w_out_ap, w_out_fourier,
              norm_ffn2, ffn2_w_gate, ffn2_w_up, ffn2_w_down, norm_final):
    y_prompt = trunk(x_prompt, meta_tokens, norm_ffn1, ffn1_w_gate, ffn1_w_up, ffn1_w_down,
                     norm_mix, w_in_ap, attn_sink, pool_w, pool_scale, w_out_ap, w_out_fourier,
                     norm_ffn2, ffn2_w_gate, ffn2_w_up, ffn2_w_down, norm_final)
    y_sample = trunk(x_sample, meta_tokens, norm_ffn1, ffn1_w_gate, ffn1_w_up, ffn1_w_down,
                     norm_mix, w_in_ap, attn_sink, pool_w, pool_scale, w_out_ap, w_out_fourier,
                     norm_ffn2, ffn2_w_gate, ffn2_w_up, ffn2_w_down, norm_final)
    return (y_prompt, y_sample)


_drawn_inputs = setup_inputs


def setup_inputs(seed=0):
    import zlib

    import numpy as np

    out = dict(_drawn_inputs(seed))
    spreads = {}
    factors = {'norm_ffn1': 5.222,
     'norm_mix': 3.657,
     'attn_sink': 60.352,
     'pool_scale': 5.024,
     'norm_ffn2': 6.078,
     'norm_final': 8.391}
    for name, (base, spread) in spreads.items():
        noise = np.random.default_rng([zlib.crc32(name.encode()), seed]).standard_normal(out[name].shape)
        drawn = base * np.exp(spread * noise) if base else spread * noise
        out[name] = __import__('jax').numpy.asarray(drawn.astype(out[name].dtype))
    for name, factor in factors.items():
        out[name] = (out[name] * factor).astype(out[name].dtype)
    return out
```

```python
from contextlib import ExitStack

import numpy as np
import concourse.bass as bass
from concourse import mybir
from concourse.alu_op_type import AluOpType as ALU

P = 128
D_MODEL, D_FF, N_META = 1024, 2816, 16
L_PROMPT, L_SAMPLE = 512 + N_META, 256 + N_META
SEQS = ((0, L_PROMPT), (L_PROMPT, L_SAMPLE))
T = L_PROMPT + L_SAMPLE
TH = T // 2
KD = D_MODEL // P
FF_TILES = D_FF // P
HALF = FF_TILES // 2
KMAX = HALF
EPS = 1e-6
N_HEADS, HEAD_DIM, WINDOW = 8, 64, 128
POOL_WINDOWS = (2, 4, 8, 16)
NEG_INF = -1e30

PAD = 8
POOL_AT = (PAD, PAD + L_PROMPT + 2 * PAD)
POOL_W = T + 4 * PAD

ATT_TILES = [(s0, L, t, min(P, L - t)) for s0, L in SEQS for t in range(0, L, P)]
KEYS = 3 * P

FT = [(106, [0, 106, 212, 318, L_PROMPT - 106]), (92, [0, 92, L_SAMPLE - 92])]
FT_TILES = [(SEQS[s][0] + t, FT[s][0], s) for s in range(2) for t in FT[s][1]]
FOLD = [L // 2 + 2 for _, L in SEQS]
NF = sum(FOLD)
GROUP = 256
DCOL = GROUP + 2
MX = 66

NORMS = ("ffn1_0", "mix_0", "ffn2_0", "ffn1_1", "mix_1", "ffn2_1", "final")

FFN_BLOCKS = 2 * (2 * HALF + KD)
N_IN = 10
N_TABLE = 4
STAGE, _n = {}, 0
for _name, _count in (("ffn1_0", FFN_BLOCKS), ("w_in", N_IN), ("w_out", KD), ("ffn2_0", FFN_BLOCKS),
                      ("ffn1_1", FFN_BLOCKS), ("tables", N_TABLE), ("w_fourier", KD),
                      ("ffn2_1", FFN_BLOCKS)):
    STAGE[_name] = _n
    _n += _count
N_BLOCKS = _n
FK = 9


def k_tiles(n):
    if n >= N_BLOCKS:
        return 0
    stage = max((s for s in STAGE if STAGE[s] <= n), key=lambda s: STAGE[s])
    at = n - STAGE[stage]
    if stage.startswith("ffn"):
        return KD if at % (2 * HALF + KD) < 2 * HALF else HALF
    return {"w_in": KD, "w_out": KD, "tables": KMAX, "w_fourier": FK}[stage]


def build(nc, x, gains, sinks, ident_in, alibi_in, edges_in, pool_w_in, tables, gate_up, down, w_in,
          w_out, w_fourier, y):
    f32, f32r = mybir.dt.float32, mybir.dt.float32r
    ACT = mybir.ActivationFunctionType
    ctx = ExitStack()

    def sb(name, shape, dt=f32):
        return ctx.enter_context(nc.sbuf_tensor(name, shape, dt))

    def scope(tensors):
        own = ExitStack()
        out = [own.enter_context(nc.sbuf_tensor(name, shape, dt)) for name, shape, dt in tensors]
        own.close()
        return out

    def sem(name):
        return ctx.enter_context(nc.semaphore(name))

    def as32(ap):
        return ap.bitcast(f32)

    h = sb("h", [P, KD, T])
    xn_hi = sb("xn_hi", [P, KD, T], f32r)
    xn_lo = sb("xn_lo", [P, KD, T], f32r)
    raw = [sb(f"raw{s}", [P, KMAX * P]) for s in range(2)]
    w_hi = [sb(f"w_hi{s}", [P, KMAX * P], f32r) for s in range(2)]
    w_lo = [sb(f"w_lo{s}", [P, KMAX * P], f32r) for s in range(2)]
    gain = sb("gain", [P, len(NORMS) * KD + 4])
    sink = sb("sink", [P, N_HEADS])
    ident = sb("ident", [P, P])
    ones = sb("ones", [P, P])
    minus_half = sb("minus_half", [P, KD])
    square = sb("square", [P, T])
    sum_sq = sb("sum_sq", [P, T])
    rstd = sb("rstd", [P, T])
    diag = sb("diag", [P, KD * 100])
    var = sb("var", [P, KD])
    rstd_tok = sb("rstd_tok", [P, KD])

    act_hi, act_lo, gate_t, up_t = scope([
        ("act_hi", [P, HALF * T], f32r), ("act_lo", [P, HALF * T], f32r),
        ("gate_t", [P, T], f32), ("up_t", [P, T], f32)])
    (q_sb, k_sb, v_sb, v_tok, u_pad, pool_a, pool_b, alibi, edges, pool_w, score, prob_t, out_tok,
     row_max, neg_max, sink_d, row_sum, sink_e, rden) = scope([
        ("q_sb", [P, 4, T], f32), ("k_sb", [P, T], f32), ("v_sb", [P, T], f32),
        ("v_tok", [P, len(ATT_TILES), P], f32), ("u_pad", [P, 4, POOL_W], f32),
        ("pool_a", [P, POOL_W], f32), ("pool_b", [P, POOL_W], f32),
        ("alibi", [P, N_HEADS, KEYS], f32), ("edges", [P, 4, 2, 2, PAD], f32),
        ("pool_w", [P, 4, P], f32), ("score", [P, 8, KEYS], f32), ("prob_t", [P, 2, KEYS], f32),
        ("out_tok", [P, 512], f32),
        ("row_max", [P, 2, 4], f32), ("neg_max", [P, 2, 4], f32), ("sink_d", [P, 2, 4], f32),
        ("row_sum", [P, 2, 8], f32), ("sink_e", [P, 2, 8], f32), ("rden", [P, 2, 8], f32)])
    (y_hi, y_lo, cs_hi, cs_lo, dft_hi, dft_lo, yx_hi, yx_lo, px_hi, px_lo, w_fold, odd) = scope([
        ("y_hi", [P, 2, 8, DCOL], f32r), ("y_lo", [P, 2, 8, DCOL], f32r),
        ("cs_hi", [P, 2 * (5 * FOLD[0] + 3 * FOLD[1])], f32r),
        ("cs_lo", [P, 2 * (5 * FOLD[0] + 3 * FOLD[1])], f32r),
        ("dft_hi", [P, 2, DCOL], f32r), ("dft_lo", [P, 2, DCOL], f32r),
        ("yx_hi", [P, 8, MX], f32r), ("yx_lo", [P, 8, MX], f32r),
        ("px_hi", [P, NF], f32r), ("px_lo", [P, NF], f32r),
        ("w_fold", [P, 8 * P], f32), ("odd", [P, NF], f32)])

    banks = ctx.enter_context(nc.psum_tensor("banks", [P, 8, 512], f32))
    AUX, STAT = 4, 6

    def slot(s, cols=TH):
        return banks[:, 2 * s:2 * s + 2, 0:cols]

    def two(ap):
        return ap.rearrange("p (b t) -> p b t", b=2)

    const_in = sem("const_in")
    h_in = [sem(f"h_in{k}") for k in range(KD)]
    mix_in = sem("mix_in")
    raw_full = [sem(f"raw_full{s}") for s in range(2)]
    w_hi_done = sem("w_hi_done")
    w_ready = sem("w_ready")
    fold_done = sem("fold_done")
    block_done = sem("block_done")
    evac_done = sem("evac_done")
    silu_done = sem("silu_done")
    prod_done = sem("prod_done")
    act_hi_done = sem("act_hi_done")
    act_ready = sem("act_ready")
    sq_done = sem("sq_done")
    xn_hi_done = sem("xn_hi_done")
    xn_ready = sem("xn_ready")
    sum_done = sem("sum_done")
    setup_done = sem("setup_done")
    stat_done = sem("stat_done")
    var_done = sem("var_done")
    rstd_tok_done = sem("rstd_tok_done")
    diag_done = sem("diag_done")
    bcast_done = sem("bcast_done")
    rstd_done = sem("rstd_done")
    y_done = sem("y_done")
    y_out = sem("y_out")

    block = ctx.enter_context(nc.Block())

    def norm_of(stage):
        return NORMS.index(stage)

    LATE_NORMS = (norm_of("ffn2_0"), norm_of("ffn2_1"))
    BCAST_NORMS = [0, 1, 2, 3, 5, 6]

    @block.sync
    def _(sp):
        def load(slot_no, n_half, source, cols, wait=True, first=False):
            if not first:
                sp.wait_ge(w_ready, n_half * 2 + slot_no - 1)
            sp.dma_start(raw[slot_no][:, 0:cols], source).then_inc(raw_full[slot_no], 16)

        def load_ffn(f, n0):
            for half in range(2):
                g0 = half * 2 * HALF
                start = n0 + half * (2 * HALF + KD)
                lo = 0
                if start == 0:
                    for s in range(2):
                        load(s, 0, gate_up[f, s], KD * P, first=True)
                    lo = 1
                with nc.sync.Fori(lo, HALF) as i:
                    for s in range(2):
                        load(s, i + start // 2, gate_up[f, bass.ds(i * 2 + (g0 + s), 1)]
                             .rearrange("o p c -> (o p) c"), KD * P)
                start += 2 * HALF
                with nc.sync.Fori(0, KD // 2) as i:
                    for s in range(2):
                        load(s, i + start // 2, down[f, bass.ds(i * 2 + (half * KD + s), 1)]
                             .rearrange("o p c -> (o p) c"), HALF * P)

        def load_stage(stage, source, cols):
            start = STAGE[stage]
            with nc.sync.Fori(0, source.shape[0] // 2) as i:
                for s in range(2):
                    load(s, i + start // 2, source[bass.ds(i * 2 + s, 1)]
                         .rearrange("o p c -> (o p) c"), cols)

        load_ffn(0, STAGE["ffn1_0"])
        sp.wait_ge(block_done, STAGE["w_in"])
        for dst, src in ((alibi, alibi_in), (edges, edges_in), (pool_w, pool_w_in)):
            sp.dma_start(dst[:].rearrange("p a b -> p (a b)") if len(dst.shape) == 3 else
                         dst[:].rearrange("p a b c d -> p (a b c d)"), src[:, :]).then_inc(mix_in, 16)
        load_stage("w_in", w_in, KD * P)
        load_stage("w_out", w_out, KD * P)
        load_ffn(1, STAGE["ffn2_0"])
        load_ffn(2, STAGE["ffn1_1"])
        load_stage("tables", tables, KMAX * P)
        load_stage("w_fourier", w_fourier, FK * P)
        load_ffn(3, STAGE["ffn2_1"])
        for k in range(KD):
            sp.wait_ge(y_done, k + 1)
            sp.dma_start(y[:, k * T:(k + 1) * T], h[:, k, :]).then_inc(y_out, 16)
        sp.wait_ge(y_out, 16 * KD)

    pad_done = sem("pad_done")
    pooled_done = sem("pooled_done")
    pool_chain = sem("pool_chain")
    v_tok_ps = sem("v_tok_ps")
    v_tok_done = sem("v_tok_done")
    score_ps = sem("score_ps")
    score_done = sem("score_done")
    neg_done = sem("neg_done")
    sinkd_done = sem("sinkd_done")
    prob_done = sem("prob_done")
    sink_e_done = sem("sink_e_done")
    prob_t_ps = sem("prob_t_ps")
    prob_t_done = sem("prob_t_done")
    head_out = sem("head_out")
    den_done = sem("den_done")
    rden_done = sem("rden_done")
    out_tok_done = sem("out_tok_done")
    out_t_ps = sem("out_t_ps")
    mix_hi_done = sem("mix_hi_done")
    mix_ready = sem("mix_ready")
    pool_ps = sem("pool_ps")
    yx_zero = sem("yx_zero")
    cd_ps = sem("cd_ps")
    cd_hi = sem("cd_hi")
    cd_done = sem("cd_done")
    yx_done = sem("yx_done")
    pd_ps = sem("pd_ps")
    pd_hi = sem("pd_hi")
    pd_done = sem("pd_done")
    odd_done = sem("odd_done")
    odd_added = sem("odd_added")

    CD_ORDER = [("cd", 0), ("cd", 1), ("pd", 0), ("cd", 2), ("pd", 1), ("cd", 3), ("pd", 2),
                ("pd", 3), ("px", 4)]

    TABLE_COLS = {1: (0, 4 * FOLD[0]), 2: (4 * FOLD[0], 8 * FOLD[0]),
                  3: (8 * FOLD[0], 10 * FOLD[0] + 6 * FOLD[1])}

    def cs_at(tile, part):
        if tile < 5:
            return (2 * tile + part) * FOLD[0]
        return 10 * FOLD[0] + (2 * (tile - 5) + part) * FOLD[1]

    UNITS = [(i, hd) for i in range(len(ATT_TILES)) for hd in range(N_HEADS)]

    def keys_of(i):
        s0, L, t, rows = ATT_TILES[i]
        return max(0, t - P), min(L, t + 2 * P)

    @block.gpsimd
    def _(pool):
        nc.gpsimd.memset(ones[:, :], 1.0).then_inc(setup_done, 1)
        nc.gpsimd.memset(minus_half[:, :], -0.5).then_inc(setup_done, 1)
        pool.wait_ge(setup_done, 2)

        def power(i):
            pool.wait_ge(var_done, i + 1)
            if i == norm_of("mix_1"):
                for s, (rows, at) in enumerate(FT):
                    c = slice(0, 5) if s == 0 else slice(5, 8)
                    last = nc.gpsimd.tensor_tensor(rstd_tok[0:rows, c], var[0:rows, c],
                                                   minus_half[0:rows, c], ALU.pow)
            else:
                last = nc.gpsimd.tensor_tensor(rstd_tok[0:100, :], var[0:100, :],
                                               minus_half[0:100, :], ALU.pow)
            last.then_inc(rstd_tok_done, 1)

        chain = [0]

        def then(ins):
            chain[0] += 1
            ins.then_inc(pool_chain, 1)
            pool.wait_ge(pool_chain, chain[0])

        power(norm_of("ffn1_0"))
        pool.wait_ge(block_done, STAGE["w_in"])
        nc.gpsimd.memset(u_pad[:, :, :], 0.0).then_inc(pad_done, 1)
        power(norm_of("mix_0"))
        pool.wait_ge(mix_in, 48)
        for g, w in enumerate(POOL_WINDOWS):
            pool.wait_ge(evac_done, STAGE["w_in"] + g + 1)
            u = u_pad[:, g, :]
            lo, hi = 1, POOL_W
            then(nc.gpsimd.tensor_tensor(pool_a[:, lo:hi], u[:, lo - 1:hi - 1], u[:, lo:hi], ALU.add))
            src, dst, size = pool_a, pool_b, 2
            while size < w:
                q = size // 2
                then(nc.gpsimd.tensor_tensor(dst[:, lo + q:hi - q], src[:, lo:hi - 2 * q],
                                             src[:, lo + 2 * q:hi], ALU.add))
                lo, hi, size = lo + q, hi - q, 2 * size
                src, dst = dst, src
            ends = (POOL_AT[0] + L_PROMPT - PAD, POOL_AT[1] + L_SAMPLE - PAD)
            for side, (a, b) in enumerate((POOL_AT, ends)):
                part = src[:, a:b + PAD].rearrange("p c -> p c")
                for s, at in enumerate((a, b)):
                    last = nc.gpsimd.tensor_tensor(src[:, at:at + PAD], src[:, at:at + PAD],
                                                   edges[:, g, s, side, :], ALU.mult)
                    if not (side and s):
                        last.then_inc(pool_chain, 1)
                        chain[0] += 1
            then(last)
            a, b = POOL_AT[0], POOL_AT[1] + L_SAMPLE
            then(nc.gpsimd.tensor_scalar(dst[:, a:b], src[:, a:b], 1.0 / w, None, ALU.mult))
            nc.gpsimd.tensor_tensor(u[:, a:b], dst[:, a:b], u[:, a:b], ALU.subtract)\
                .then_inc(pooled_done, 1)
            pool.wait_ge(pooled_done, g + 1)
        power(norm_of("ffn2_0"))
        power(norm_of("ffn1_1"))
        pool.wait_ge(block_done, STAGE["tables"])
        nc.gpsimd.memset(as32(yx_hi[:, :, :]), 0.0).then_inc(yx_zero, 1)
        nc.gpsimd.memset(as32(yx_lo[:, :, :]), 0.0).then_inc(yx_zero, 1)
        power(norm_of("mix_1"))
        pool.wait_ge(yx_zero, 2)

        def fold(n):
            pool.wait_ge(raw_full[n % 2], 16 * (n // 2 + 1))
            pool.wait_ge(w_ready, n)
            a, b = raw[n % 2][:, 0:4 * P], raw[n % 2][:, 4 * P:8 * P]
            nc.gpsimd.tensor_tensor(w_fold[:, 0:4 * P], a, b, ALU.add).then_inc(fold_done, 1)
            nc.gpsimd.tensor_tensor(w_fold[:, 4 * P:8 * P], b, a, ALU.subtract).then_inc(fold_done, 1)

        cd = 0
        for kind, g in CD_ORDER:
            if kind == "cd":
                cd += 1
                pool.wait_ge(cd_done, 8 * cd)
                for (dst, src) in ((yx_hi, y_hi), (yx_lo, y_lo)):
                    for s, (rows, _) in enumerate(FT):
                        c = slice(0, 5) if s == 0 else slice(5, 8)
                        last = nc.gpsimd.tensor_copy(dst[0:rows, c, g:g + 1],
                                                     src[0:rows, g % 2, c, GROUP:GROUP + 1])
                        last.then_inc(yx_done, 1)
        nf = STAGE["w_fourier"]
        for n in (nf, nf + 1):
            fold(n)
        for m in range(KD):
            n = nf + m
            pool.wait_ge(odd_done, m + 1)
            c0 = 0
            for s, (s0, L) in enumerate(SEQS):
                half = L // 2 + 1
                fwd = h[:, m, s0:s0 + half]
                bwd = h[:, m, s0 + half:s0 + L]
                nc.gpsimd.tensor_tensor(fwd, fwd, odd[:, c0:c0 + half], ALU.add)\
                    .then_inc(odd_added, 1)
                nc.gpsimd.tensor_tensor(bwd, bwd, odd[:, c0 + half - 2:c0:-1], ALU.subtract)\
                    .then_inc(odd_added, 1)
                c0 += FOLD[s]
            if m + 2 < KD:
                fold(n + 2)
        power(norm_of("ffn2_1"))
        power(norm_of("final"))

    @block.scalar
    def _(act):
        A = nc.scalar

        def split_hi(s, n, n_half, k, first=False):
            act.wait_ge(raw_full[s], (n_half + 1) * 16)
            if not first:
                act.wait_ge(block_done, n_half * 2 + s - 1)
            A.activation(w_hi[s][:, 0:k * P], raw[s][:, 0:k * P], ACT.Copy).then_inc(w_hi_done, 1)

        def split_hi_static(n):
            if n >= N_BLOCKS:
                return
            s, stage_t, stage_f = n % 2, STAGE["tables"], STAGE["w_fourier"]
            if stage_t <= n < stage_f:
                act.wait_ge(raw_full[s], 16 * (n // 2 + 1))
                act.wait_ge(block_done, stage_t)
                r = n - stage_t
                if r == 0:
                    A.activation(dft_hi[:, :, :], raw[s][:, 0:2 * DCOL].rearrange("p (a b) -> p a b", a=2),
                                 ACT.Copy).then_inc(w_hi_done, 1)
                else:
                    a, b = TABLE_COLS[r]
                    rows = FT[0][0]
                    A.activation(cs_hi[0:rows, a:b], raw[s][0:rows, 0:b - a], ACT.Copy)\
                        .then_inc(w_hi_done, 1)
            elif stage_f <= n < stage_f + KD:
                act.wait_ge(block_done, n - 1)
                act.wait_ge(fold_done, 2 * (n - stage_f) + 2)
                A.activation(w_hi[s][:, 0:8 * P], w_fold[:, :], ACT.Copy)
                A.activation(w_hi[s][:, 8 * P:9 * P], raw[s][:, 8 * P:9 * P], ACT.Copy)\
                    .then_inc(w_hi_done, 1)
            else:
                split_hi(s, n, n // 2, k_tiles(n), first=n < 2)

        def gain_hi(i, m):
            A.activation(xn_hi[:, m, :], h[:, m, :], ACT.Copy,
                         scale=gain[:, i * KD + m:i * KD + m + 1]).then_inc(xn_hi_done, 1)

        def norm_hi(i, m):
            if i < len(NORMS) - 1 and i not in LATE_NORMS:
                gain_hi(i, m)
            act.wait_ge(sum_done, 9 * i + m + 1)
            A.activation(square[:, :], h[:, m, :], ACT.Square).then_inc(sq_done, 1)

        def ffn(f, stage, norm_after):
            n0 = STAGE[stage]
            j0 = f * FF_TILES
            for half in range(2):
                b0 = n0 + half * (2 * HALF + KD)
                jj = j0 + half * HALF

                def pair(i, nxt):
                    act.wait_ge(block_done, i * 2 + (b0 + 1))
                    nxt(0)
                    act.wait_ge(evac_done, i * 2 + (b0 + 1))
                    A.activation(gate_t[:, :], gate_t[:, :], ACT.Silu).then_inc(silu_done, 1)
                    act.wait_ge(block_done, i * 2 + (b0 + 2))
                    nxt(1)
                    act.wait_ge(prod_done, i + (jj + 1))
                    A.activation(act_hi[:, bass.ds(i * T, T)], up_t[:, :], ACT.Copy)\
                        .then_inc(act_hi_done, 1)

                with A.Fori(0, HALF - 1) as i:
                    pair(i, lambda s: split_hi(s, None, i + (b0 // 2 + 1), KD))
                last = b0 + 2 * (HALF - 1)
                pair(HALF - 1, lambda s: split_hi_static(last + 2 + s))
                d0 = b0 + 2 * HALF
                for m in range(KD):
                    act.wait_ge(block_done, d0 + m + 1)
                    split_hi_static(d0 + m + 2)
                    if half:
                        act.wait_ge(evac_done, d0 + m + 1)
                        norm_hi(norm_after, m)

        for k in range(KD):
            act.dma_start(h[:, k, :], x[:, k * T:(k + 1) * T]).then_inc(h_in[k], 16)
            if k == 0:
                for dst, src in ((gain, gains), (sink, sinks), (ident, ident_in)):
                    act.dma_start(dst[:, :], src[:, :]).then_inc(const_in, 16)
        split_hi_static(0)
        act.wait_ge(const_in, 48)
        for m in range(KD):
            act.wait_ge(h_in[m], 16)
            norm_hi(0, m)
            if m == 0:
                split_hi_static(1)
        ffn(0, "ffn1_0", norm_of("mix_0"))

        b0 = STAGE["w_in"]
        for r in range(N_IN):
            act.wait_ge(block_done, b0 + r + 1)
            split_hi_static(b0 + r + 2)
        for i, (s0, L, t, rows) in enumerate(ATT_TILES):
            act.wait_ge(v_tok_ps, i + 1)
            A.activation(v_tok[0:rows, i, :], banks[0:rows, 6 + i % 2, 0:P], ACT.Copy)\
                .then_inc(v_tok_done, 1)

        def exp_quad(q):
            i = q // 2
            rows = ATT_TILES[i][3]
            k0, k1 = keys_of(i)
            act.wait_ge(neg_done, q + 1)
            if i >= 2:
                act.wait_ge(rden_done, i - 1)
            for c in range(4):
                u = 4 * q + c
                A.activation(score[0:rows, u % 8, 0:k1 - k0], score[0:rows, u % 8, 0:k1 - k0],
                             ACT.Exp, bias=neg_max[0:rows, q % 2, c:c + 1],
                             accum_out=row_sum[0:rows, i % 2, u % 8:u % 8 + 1]).then_inc(prob_done, 1)
            act.wait_ge(sinkd_done, q + 1)
            hb = 4 * (q % 2)
            A.activation(sink_e[0:rows, i % 2, hb:hb + 4], sink_d[0:rows, q % 2, :], ACT.Exp)\
                .then_inc(sink_e_done, 1)

        def prob_copy(u):
            i = u // 8
            rows = ATT_TILES[i][3]
            k0, k1 = keys_of(i)
            act.wait_ge(prob_t_ps, u + 1)
            if u >= 2:
                act.wait_ge(head_out, u - 1)
            for j in range((k1 - k0 + P - 1) // P):
                kr = min(P, k1 - k0 - j * P)
                if kr < P:
                    A.activation(prob_t[0:kr, u % 2, j * P:j * P + rows],
                                 banks[0:kr, 3 + u % 2, j * P:j * P + rows], ACT.Copy)\
                        .then_inc(prob_t_done, 1)
            full = (k1 - k0) // P
            A.activation(prob_t[:, u % 2, 0:full * P].rearrange("p (j r) -> p j r", r=P)[:, :, 0:rows],
                         banks[:, 3 + u % 2, 0:full * P].rearrange("p (j r) -> p j r", r=P)[:, :, 0:rows],
                         ACT.Copy).then_inc(prob_t_done, 1)

        def out_hi(i):
            s0, L, t, rows = ATT_TILES[i]
            act.wait_ge(out_t_ps, i + 1)
            A.activation(xn_hi[:, 0:4, s0 + t:s0 + t + rows],
                         banks[:, 6, :].rearrange("p (k r) -> p k r", k=4)[:, :, 0:rows],
                         ACT.Copy).then_inc(mix_hi_done, 1)

        NQ = len(ATT_TILES) * 2
        for q in range(NQ + 1):
            if q < NQ:
                exp_quad(q)
            if q >= 1:
                for c in range(4):
                    prob_copy(4 * (q - 1) + c)
                if q >= 3 and q % 2 == 1:
                    out_hi((q - 3) // 2)
        out_hi(len(ATT_TILES) - 1)
        for g in range(4):
            act.wait_ge(pool_ps, g + 1)
            sc = gain[:, len(NORMS) * KD + g:len(NORMS) * KD + g + 1]
            A.activation(two(xn_hi[:, 4 + g, :]), slot(g % 2), ACT.Copy, scale=sc)\
                .then_inc(mix_hi_done, 1)
        b0 = STAGE["w_out"]
        for m in range(KD):
            act.wait_ge(block_done, b0 + m + 1)
            split_hi_static(b0 + m + 2)
            act.wait_ge(evac_done, b0 + m + 1)
            norm_hi(norm_of("ffn2_0"), m)
        for m in range(KD):
            gain_hi(norm_of("ffn2_0"), m)
        ffn(1, "ffn2_0", norm_of("ffn1_1"))
        ffn(2, "ffn1_1", norm_of("mix_1"))

        nt = STAGE["tables"]
        split_hi_static(nt + 2)
        split_hi_static(nt + 3)
        act.wait_ge(rstd_tok_done, norm_of("mix_1") + 1)
        cd = pd = 0
        for kind, g in CD_ORDER:
            if kind == "cd":
                for i, (t0, rows, s) in enumerate(FT_TILES):
                    act.wait_ge(cd_ps, cd + 1)
                    if g >= 2 and i == 0:
                        act.wait_ge(yx_done, 4 * (g - 1))
                    A.activation(y_hi[0:rows, g % 2, i, :], banks[0:rows, cd % 4, 0:DCOL], ACT.Copy,
                                 scale=rstd_tok[0:rows, i:i + 1]).then_inc(cd_hi, 1)
                    cd += 1
            elif kind == "pd":
                for part in range(2):
                    act.wait_ge(pd_ps, pd + 1)
                    A.activation(xn_hi[:, 2 * g + part, 0:NF], banks[:, 4 + pd % 4, 0:NF], ACT.Copy)\
                        .then_inc(pd_hi, 1)
                    pd += 1
            else:
                act.wait_ge(pd_ps, pd + 1)
                A.activation(px_hi[0:MX, :], banks[0:MX, 4 + pd % 4, 0:NF], ACT.Copy)\
                    .then_inc(pd_hi, 1)
        nf = STAGE["w_fourier"]
        split_hi_static(nf)
        split_hi_static(nf + 1)
        for m in range(KD):
            act.wait_ge(block_done, nf + m + 1)
            if m:
                act.wait_ge(odd_added, 4 * m)
            A.activation(odd[:, :], banks[:, 2 * (m % 2) + 1, 0:NF], ACT.Copy).then_inc(odd_done, 1)
            split_hi_static(nf + m + 2)
            act.wait_ge(evac_done, nf + m + 1)
            norm_hi(norm_of("ffn2_1"), m)
        for m in range(KD):
            gain_hi(norm_of("ffn2_1"), m)
        ffn(3, "ffn2_1", norm_of("final"))

    @block.vector
    def _(dve):
        V = nc.vector

        def split_lo(s, n_half, k):
            dve.wait_ge(w_hi_done, n_half * 2 + (s + 1))
            V.tensor_tensor(w_lo[s][:, 0:k * P], raw[s][:, 0:k * P], as32(w_hi[s][:, 0:k * P]),
                            ALU.subtract).then_inc(w_ready, 1)

        def split_lo_static(n):
            if n >= N_BLOCKS:
                return
            s, stage_t, stage_f = n % 2, STAGE["tables"], STAGE["w_fourier"]
            if stage_t <= n < stage_f:
                dve.wait_ge(w_hi_done, n + 1)
                r = n - stage_t
                if r == 0:
                    V.tensor_tensor(dft_lo[:, :, :], raw[s][:, 0:2 * DCOL].rearrange("p (a b) -> p a b", a=2),
                                    as32(dft_hi[:, :, :]), ALU.subtract).then_inc(w_ready, 1)
                else:
                    a, b = TABLE_COLS[r]
                    rows = FT[0][0]
                    V.tensor_tensor(cs_lo[0:rows, a:b], raw[s][0:rows, 0:b - a],
                                    as32(cs_hi[0:rows, a:b]), ALU.subtract).then_inc(w_ready, 1)
            elif stage_f <= n < stage_f + KD:
                dve.wait_ge(w_hi_done, n + 1)
                V.tensor_tensor(w_lo[s][:, 0:8 * P], w_fold[:, :], as32(w_hi[s][:, 0:8 * P]),
                                ALU.subtract)
                V.tensor_tensor(w_lo[s][:, 8 * P:9 * P], raw[s][:, 8 * P:9 * P],
                                as32(w_hi[s][:, 8 * P:9 * P]), ALU.subtract).then_inc(w_ready, 1)
            else:
                split_lo(s, n // 2, k_tiles(n))

        def gain_lo(i, m):
            dve.wait_ge(xn_hi_done, i * KD + m + 1)
            V.scalar_tensor_tensor(xn_lo[:, m, :], h[:, m, :],
                                   gain[:, i * KD + m:i * KD + m + 1], as32(xn_hi[:, m, :]),
                                   ALU.mult, ALU.subtract).then_inc(xn_ready, 1)

        def norm_lo(i, m):
            if i < len(NORMS) - 1 and i not in LATE_NORMS:
                gain_lo(i, m)
            dve.wait_ge(sq_done, i * KD + m + 1)
            dve.wait_ge(sum_done, 9 * i + m + 1)
            V.tensor_tensor(sum_sq[:, :], sum_sq[:, :], square[:, :], ALU.add).then_inc(sum_done, 1)

        def variance(i):
            dve.wait_ge(stat_done, i + 1)
            if i == norm_of("mix_1"):
                for s, (rows, at) in enumerate(FT):
                    c = slice(0, 5) if s == 0 else slice(5, 8)
                    last = V.tensor_scalar(var[0:rows, c], banks[0:rows, STAT, c], 1.0 / D_MODEL,
                                           EPS, ALU.mult, ALU.add)
                    if s == 0:
                        last.then_inc(evac_done, N_TABLE)
            else:
                last = V.tensor_scalar(var[0:100, :], banks[0:100, STAT, 0:KD], 1.0 / D_MODEL, EPS,
                                       ALU.mult, ALU.add)
            last.then_inc(var_done, 1)
            if i < len(NORMS) - 1:
                V.memset(sum_sq[:, :], 0.0).then_inc(sum_done, 1)

        def diagonal(i):
            dve.wait_ge(rstd_tok_done, i + 1)
            V.tensor_tensor(diag[0:100, :].rearrange("p (k t) -> p k t", k=KD),
                            ident[0:100, None, 0:100].to_broadcast([100, KD, 100]),
                            rstd_tok[0:100, :, None].to_broadcast([100, KD, 100]),
                            ALU.mult).then_inc(diag_done, 1)

        def spread(i):
            b = BCAST_NORMS.index(i) + 1
            if i not in LATE_NORMS:
                diagonal(i)
            dve.wait_ge(bcast_done, b)
            V.tensor_copy(two(rstd[:, :]), banks[:, AUX:AUX + 2, 0:TH]).then_inc(rstd_done, 1)
            dve.wait_ge(rstd_done, b)

        def ffn(f, stage, norm_after, norm_before):
            n0 = STAGE[stage]
            j0 = f * FF_TILES
            for half in range(2):
                b0 = n0 + half * (2 * HALF + KD)
                jj = j0 + half * HALF

                def pair(i, nxt):
                    dve.wait_ge(block_done, i * 2 + (b0 + 1))
                    V.tensor_tensor(two(gate_t[:, :]), slot(0), two(rstd[:, :]), ALU.mult)\
                        .then_inc(evac_done, 1)
                    nxt(0)
                    dve.wait_ge(block_done, i * 2 + (b0 + 2))
                    dve.wait_ge(evac_done, i * 2 + (b0 + 1))
                    V.tensor_tensor(two(up_t[:, :]), slot(1), two(rstd[:, :]), ALU.mult)\
                        .then_inc(evac_done, 1)
                    dve.wait_ge(silu_done, i + (jj + 1))
                    dve.wait_ge(evac_done, i * 2 + (b0 + 2))
                    V.tensor_tensor(up_t[:, :], up_t[:, :], gate_t[:, :], ALU.mult)\
                        .then_inc(prod_done, 1)
                    nxt(1)
                    dve.wait_ge(act_hi_done, i + (jj + 1))
                    V.tensor_tensor(act_lo[:, bass.ds(i * T, T)], up_t[:, :],
                                    as32(act_hi[:, bass.ds(i * T, T)]), ALU.subtract)\
                        .then_inc(act_ready, 1)

                if half == 0:
                    variance(norm_before)
                    for m in range(KD if norm_before in LATE_NORMS else 0):
                        if m == 2:
                            diagonal(norm_before)
                        gain_lo(norm_before, m)
                    spread(norm_before)
                with V.Fori(0, HALF - 1) as i:
                    pair(i, lambda s: split_lo(s, i + (b0 // 2 + 1), KD))
                last = b0 + 2 * (HALF - 1)
                pair(HALF - 1, lambda s: split_lo_static(last + 2 + s))
                d0 = b0 + 2 * HALF
                for m in range(KD):
                    dve.wait_ge(block_done, d0 + m + 1)
                    V.scalar_tensor_tensor(two(h[:, m, :]), slot(m % 2), 0.5, two(h[:, m, :]),
                                           ALU.mult, ALU.add).then_inc(evac_done, 1)
                    if half:
                        norm_lo(norm_after, m)
                    split_lo_static(d0 + m + 2)

        V.memset(sum_sq[:, :], 0.0).then_inc(sum_done, 1)
        split_lo_static(0)
        dve.wait_ge(const_in, 48)
        for m in range(KD):
            dve.wait_ge(h_in[m], 16)
            norm_lo(0, m)
            if m == 0:
                split_lo_static(1)
        ffn(0, "ffn1_0", norm_of("mix_0"), norm_of("ffn1_0"))

        b0 = STAGE["w_in"]
        variance(norm_of("mix_0"))
        spread(norm_of("mix_0"))
        dve.wait_ge(pad_done, 1)
        for r in range(N_IN):
            s = r % 2
            dve.wait_ge(block_done, b0 + r + 1)
            if r < 4:
                cut = L_PROMPT - TH
                V.tensor_tensor(u_pad[:, r, PAD:PAD + TH], banks[:, 2 * s, 0:TH], rstd[:, 0:TH],
                                ALU.mult)
                V.tensor_tensor(u_pad[:, r, PAD + TH:PAD + L_PROMPT], banks[:, 2 * s + 1, 0:cut],
                                rstd[:, TH:L_PROMPT], ALU.mult)
                V.tensor_tensor(u_pad[:, r, POOL_AT[1]:POOL_AT[1] + L_SAMPLE],
                                banks[:, 2 * s + 1, cut:TH], rstd[:, L_PROMPT:T],
                                ALU.mult).then_inc(evac_done, 1)
            elif r < 6:
                dst = v_sb if r == 4 else k_sb
                V.tensor_tensor(two(dst[:, :]), slot(s), two(rstd[:, :]), ALU.mult)\
                    .then_inc(evac_done, 1)
            else:
                V.scalar_tensor_tensor(two(q_sb[:, r - 6, :]), slot(s), HEAD_DIM ** -0.5,
                                       two(rstd[:, :]), ALU.mult, ALU.mult).then_inc(evac_done, 1)
            split_lo_static(b0 + r + 2)
        dve.wait_ge(mix_in, 48)

        def score_quad(q):
            i = q // 2
            rows = ATT_TILES[i][3]
            k0, k1 = keys_of(i)
            off = k0 - (ATT_TILES[i][2] - P)
            for c in range(4):
                u = 4 * q + c
                hd = u % 8
                dve.wait_ge(score_ps, u + 1)
                if u >= 8:
                    dve.wait_ge(prob_t_ps, u - 7)
                V.tensor_tensor_reduce(out=score[0:rows, hd, 0:k1 - k0],
                                       in0=banks[0:rows, u % 3, 0:k1 - k0],
                                       in1=alibi[0:rows, hd, off:off + k1 - k0], scale=1.0,
                                       scalar=sink[0:rows, hd:hd + 1], op0=ALU.add, op1=ALU.max,
                                       accum_out=row_max[0:rows, q % 2, c:c + 1])\
                    .then_inc(score_done, 1)
            dve.wait_ge(score_done, 4 * q + 4)
            if q >= 2:
                dve.wait_ge(sink_e_done, q - 1)
            V.tensor_scalar(neg_max[0:rows, q % 2, :], row_max[0:rows, q % 2, :], -1.0, None,
                            ALU.mult).then_inc(neg_done, 1)
            dve.wait_ge(neg_done, q + 1)
            hb = 4 * (q % 2)
            V.tensor_tensor(sink_d[0:rows, q % 2, :], sink[0:rows, hb:hb + 4],
                            neg_max[0:rows, q % 2, :], ALU.add).then_inc(sinkd_done, 1)

        def tile_out(i):
            s0, L, t, rows = ATT_TILES[i]
            dve.wait_ge(prob_done, 8 * i + 8)
            dve.wait_ge(sink_e_done, 2 * i + 2)
            V.tensor_tensor(rden[0:rows, i % 2, :], row_sum[0:rows, i % 2, :],
                            sink_e[0:rows, i % 2, :], ALU.add).then_inc(den_done, 1)
            dve.wait_ge(den_done, i + 1)
            V.reciprocal(rden[0:rows, i % 2, :], rden[0:rows, i % 2, :]).then_inc(rden_done, 1)
            dve.wait_ge(rden_done, i + 1)
            dve.wait_ge(head_out, 8 * i + 8)
            if i:
                dve.wait_ge(out_t_ps, i)
            V.tensor_tensor(out_tok[0:rows, :].rearrange("p (a b) -> p a b", a=8),
                            banks[0:rows, 5, :].rearrange("p (a b) -> p a b", a=8),
                            rden[0:rows, i % 2, :, None].to_broadcast([rows, 8, HEAD_DIM]),
                            ALU.mult).then_inc(out_tok_done, 1)

        def tile_lo(i):
            s0, L, t, rows = ATT_TILES[i]
            dve.wait_ge(mix_hi_done, i + 1)
            V.tensor_tensor(xn_lo[:, 0:4, s0 + t:s0 + t + rows],
                            banks[:, 6, :].rearrange("p (k r) -> p k r", k=4)[:, :, 0:rows],
                            as32(xn_hi[:, 0:4, s0 + t:s0 + t + rows]),
                            ALU.subtract).then_inc(mix_ready, 1)

        NQ = len(ATT_TILES) * 2
        for q in range(NQ):
            score_quad(q)
            if q >= 3 and q % 2 == 1:
                tile_out((q - 3) // 2)
            if q >= 4 and q % 2 == 0:
                tile_lo((q - 4) // 2)
        tile_lo(len(ATT_TILES) - 2)
        tile_out(len(ATT_TILES) - 1)
        tile_lo(len(ATT_TILES) - 1)
        for g in range(4):
            sc = gain[:, len(NORMS) * KD + g:len(NORMS) * KD + g + 1]
            dve.wait_ge(mix_hi_done, len(ATT_TILES) + g + 1)
            V.scalar_tensor_tensor(two(xn_lo[:, 4 + g, :]), slot(g % 2), sc,
                                   two(as32(xn_hi[:, 4 + g, :])), ALU.mult, ALU.subtract)\
                .then_inc(mix_ready, 1)
        b0 = STAGE["w_out"]
        for m in range(KD):
            dve.wait_ge(block_done, b0 + m + 1)
            V.tensor_tensor(two(h[:, m, :]), slot(m % 2), two(h[:, m, :]), ALU.add)\
                .then_inc(evac_done, 1)
            norm_lo(norm_of("ffn2_0"), m)
            split_lo_static(b0 + m + 2)
        ffn(1, "ffn2_0", norm_of("ffn1_1"), norm_of("ffn2_0"))
        ffn(2, "ffn1_1", norm_of("mix_1"), norm_of("ffn1_1"))

        nt = STAGE["tables"]
        variance(norm_of("mix_1"))
        split_lo_static(nt + 2)
        split_lo_static(nt + 3)
        cd = pd = 0
        for kind, g in CD_ORDER:
            if kind == "cd":
                for i, (t0, rows, s) in enumerate(FT_TILES):
                    dve.wait_ge(cd_hi, cd + 1)
                    V.scalar_tensor_tensor(y_lo[0:rows, g % 2, i, :], banks[0:rows, cd % 4, 0:DCOL],
                                           rstd_tok[0:rows, i:i + 1], as32(y_hi[0:rows, g % 2, i, :]),
                                           ALU.mult, ALU.subtract).then_inc(cd_done, 1)
                    cd += 1
            elif kind == "pd":
                for part in range(2):
                    dve.wait_ge(pd_hi, pd + 1)
                    V.tensor_tensor(xn_lo[:, 2 * g + part, 0:NF], banks[:, 4 + pd % 4, 0:NF],
                                    as32(xn_hi[:, 2 * g + part, 0:NF]), ALU.subtract)\
                        .then_inc(pd_done, 1)
                    pd += 1
            else:
                dve.wait_ge(pd_hi, pd + 1)
                V.tensor_tensor(px_lo[0:MX, :], banks[0:MX, 4 + pd % 4, 0:NF],
                                as32(px_hi[0:MX, :]), ALU.subtract).then_inc(pd_done, 1)
        nf = STAGE["w_fourier"]
        split_lo_static(nf)
        split_lo_static(nf + 1)
        for m in range(KD):
            dve.wait_ge(odd_added, 4 * m + 4)
            even = banks[:, 2 * (m % 2), :]
            c0 = 0
            for s, (s0, L) in enumerate(SEQS):
                half = L // 2 + 1
                fwd = h[:, m, s0:s0 + half]
                bwd = h[:, m, s0 + half:s0 + L]
                V.tensor_tensor(fwd, even[:, c0:c0 + half], fwd, ALU.add)
                last = V.tensor_tensor(bwd, even[:, c0 + half - 2:c0:-1], bwd, ALU.add)
                c0 += FOLD[s]
            last.then_inc(evac_done, 1)
            norm_lo(norm_of("ffn2_1"), m)
            split_lo_static(nf + m + 2)
        ffn(3, "ffn2_1", norm_of("final"), norm_of("ffn2_1"))
        variance(norm_of("final"))
        spread(norm_of("final"))
        for m in range(KD):
            i = norm_of("final")
            V.scalar_tensor_tensor(h[:, m, :], h[:, m, :], gain[:, i * KD + m:i * KD + m + 1],
                                   rstd[:, :], ALU.mult, ALU.mult).then_inc(y_done, 1)

    @block.tensor
    def _(pe):
        M = nc.tensor

        def triple(out, lhs, rhs, first, last, opening=None):
            (a_hi, a_lo), (b_hi, b_lo) = lhs, rhs
            for j, (a, b) in enumerate(((a_hi, b_hi), (a_hi, b_lo), (a_lo, b_hi))):
                ins = M.matmul(out, a, b, start=first and j == 0, stop=last and j == 2)
                if opening and j == 0:
                    ins.then_inc(*opening)
            return ins

        def token_halves(s, lhs, rhs_hi, rhs_lo, first, last):
            for j, (a, b) in enumerate(((lhs[0], rhs_hi), (lhs[0], rhs_lo), (lhs[1], rhs_hi))):
                for half in range(2):
                    ins = M.matmul(banks[:, 2 * s + half, 0:TH], a, b[:, half * TH:(half + 1) * TH],
                                   start=first and j == 0, stop=last and j == 2)
            return ins

        def open_block(s, n_half):
            pe.wait_ge(w_ready, n_half * 2 + (s + 1))
            if not (isinstance(n_half, int) and n_half == 0):
                pe.wait_ge(evac_done, n_half * 2 + (s - 1))

        def run_block(s, k, rhs, before=None):
            for kt in range(k):
                if before:
                    before(kt)
                lhs = (w_hi[s][:, kt * P:(kt + 1) * P], w_lo[s][:, kt * P:(kt + 1) * P])
                ins = token_halves(s, lhs, *rhs(kt), kt == 0, kt == k - 1)
            ins.then_inc(block_done, 1)

        def xn(kt):
            return xn_hi[:, kt, :], xn_lo[:, kt, :]

        def act_part(kt):
            return act_hi[:, kt * T:(kt + 1) * T], act_lo[:, kt * T:(kt + 1) * T]

        def statistics(i):
            pe.wait_ge(sum_done, 9 * i + 9)
            pe.wait_ge(setup_done, 2)
            tiles = [(100 * k, 100) for k in range(KD)]
            if i == norm_of("mix_1"):
                tiles = [(t0, rows) for t0, rows, _ in FT_TILES]
            for k, (t0, rows) in enumerate(tiles):
                ins = M.matmul(banks[0:rows, STAT, k:k + 1], sum_sq[:, t0:t0 + rows], ones[:, 0:1],
                               start=True, stop=True)
            ins.then_inc(stat_done, 1)

        def broadcast(i):
            pe.wait_ge(diag_done, BCAST_NORMS.index(i) + 1)
            for half in range(2):
                ins = M.matmul(banks[:, AUX + half, 0:TH], ones[0:100, :],
                               diag[0:100, half * TH:(half + 1) * TH], start=True, stop=True)
            ins.then_inc(bcast_done, 1)

        def first_blocks(n, i):
            if i in LATE_NORMS:
                statistics(i)
                open_block(0, n // 2)
                open_block(1, n // 2)
                for kt in range(KD):
                    pe.wait_ge(xn_ready, i * KD + kt + 1)
                    if kt == 4:
                        broadcast(i)
                    for s in range(2):
                        lhs = (w_hi[s][:, kt * P:(kt + 1) * P], w_lo[s][:, kt * P:(kt + 1) * P])
                        ins = token_halves(s, lhs, *xn(kt), kt == 0, kt == KD - 1)
                        if kt == KD - 1:
                            ins.then_inc(block_done, 1)
                return
            open_block(0, n // 2)
            run_block(0, KD, xn, lambda kt: pe.wait_ge(xn_ready, i * KD + kt + 1))
            statistics(i)
            open_block(1, n // 2)
            run_block(1, KD, xn, lambda kt: broadcast(i) if kt == 4 else None)

        def ffn(f, stage, norm_before):
            n0 = STAGE[stage]
            for half in range(2):
                b0 = n0 + half * (2 * HALF + KD)
                if half == 0:
                    first_blocks(b0, norm_before)
                with M.Fori(1 - half, HALF) as i:
                    for s in range(2):
                        open_block(s, i + b0 // 2)
                        run_block(s, KD, xn)
                d0 = b0 + 2 * HALF
                jj = f * FF_TILES + half * HALF
                pe.wait_ge(act_ready, jj + HALF - 1)
                with M.Fori(0, KD // 2) as i:
                    for s in range(2):
                        open_block(s, i + d0 // 2)
                        run_block(s, HALF, act_part, lambda kt: pe.wait_ge(act_ready, jj + HALF)
                                  if kt == HALF - 1 and s == 0 else None)

        def stage_blocks(stage, lo=0, count=KD, before=None):
            b0 = STAGE[stage]
            with M.Fori(lo // 2, count // 2) as i:
                for s in range(2):
                    open_block(s, i + b0 // 2)
                    run_block(s, KD, xn)

        pe.wait_ge(const_in, 48)
        ffn(0, "ffn1_0", norm_of("ffn1_0"))

        b0 = STAGE["w_in"]
        first_blocks(b0, norm_of("mix_0"))
        stage_blocks("w_in", 2, N_IN)
        pe.wait_ge(evac_done, b0 + N_IN)
        for i, (s0, L, t, rows) in enumerate(ATT_TILES):
            if i >= 2:
                pe.wait_ge(v_tok_done, i - 1)
            M.transpose(banks[0:rows, 6 + i % 2, 0:P], v_sb[:, s0 + t:s0 + t + rows], ident[:, :])\
                .then_inc(v_tok_ps, 1)

        def scores(u):
            i, hd = UNITS[u]
            s0, L, t, rows = ATT_TILES[i]
            k0, k1 = keys_of(i)
            side = 64 * (hd // 4)
            if u >= 3:
                pe.wait_ge(score_done, u - 2)
            M.matmul(banks[0:rows, u % 3, 0:k1 - k0],
                     q_sb[side:side + 64, hd % 4, s0 + t:s0 + t + rows],
                     k_sb[side:side + 64, s0 + k0:s0 + k1], start=True, stop=True)\
                .then_inc(score_ps, 1)

        def transposes(u):
            i, hd = UNITS[u]
            rows = ATT_TILES[i][3]
            k0, k1 = keys_of(i)
            pe.wait_ge(prob_done, u + 1)
            if u >= 2:
                pe.wait_ge(prob_t_done, TCOUNT[u - 1])
            for j in range((k1 - k0 + P - 1) // P):
                kr = min(P, k1 - k0 - j * P)
                ins = M.transpose(banks[0:kr, 3 + u % 2, j * P:j * P + rows],
                                  score[0:rows, hd, j * P:j * P + kr], ident[0:rows, 0:rows])
            ins.then_inc(prob_t_ps, 1)

        def times_v(u):
            i, hd = UNITS[u]
            s0, L, t, rows = ATT_TILES[i]
            k0, k1 = keys_of(i)
            side = 64 * (hd // 4)
            pe.wait_ge(prob_t_done, TCOUNT[u + 1])
            if u == 0:
                pe.wait_ge(v_tok_done, len(ATT_TILES))
            if hd == 0 and i:
                pe.wait_ge(out_tok_done, i)
            n = (k1 - k0 + P - 1) // P
            tile0 = i - t // P + k0 // P
            for j in range(n):
                kr = min(P, k1 - k0 - j * P)
                ins = M.matmul(banks[0:rows, 5, hd * 64:hd * 64 + 64],
                               prob_t[0:kr, u % 2, j * P:j * P + rows],
                               v_tok[0:kr, tile0 + j, side:side + 64], start=j == 0, stop=j == n - 1)
            ins.then_inc(head_out, 1)

        def out_back(i):
            s0, L, t, rows = ATT_TILES[i]
            pe.wait_ge(out_tok_done, i + 1)
            if i:
                pe.wait_ge(mix_ready, i)
            for k in range(4):
                ins = M.transpose(banks[:, 6, k * P:k * P + rows], out_tok[0:rows, k * P:(k + 1) * P],
                                  ident[0:rows, 0:rows])
            ins.then_inc(out_t_ps, 1)

        TCOUNT = [0]
        for i, hd in UNITS:
            k0, k1 = keys_of(i)
            TCOUNT.append(TCOUNT[-1] + (2 if (k1 - k0) % P else 1))
        NU = len(UNITS)
        AHEAD = 6
        for u in range(NU + AHEAD + 1):
            if u < NU:
                scores(u)
            v = u - AHEAD
            if 0 <= v < NU:
                transposes(v)
            if 1 <= v <= NU:
                times_v(v - 1)
                if v % 8 == 3 and v > 8:
                    out_back(v // 8 - 1)
        out_back(len(ATT_TILES) - 1)
        for g in range(4):
            pe.wait_ge(pooled_done, g + 1)
            if g == 0:
                pe.wait_ge(mix_in, 48)
                pe.wait_ge(score_done, NU)
                pe.wait_ge(prob_t_done, TCOUNT[-1])
            if g >= 2:
                pe.wait_ge(mix_ready, len(ATT_TILES) + g - 1)
            cut = L_PROMPT - TH
            s = g % 2
            M.matmul(banks[:, 2 * s, 0:TH], pool_w[:, g, :], u_pad[:, g, PAD:PAD + TH],
                     start=True, stop=True)
            M.matmul(banks[:, 2 * s + 1, 0:cut], pool_w[:, g, :],
                     u_pad[:, g, PAD + TH:PAD + L_PROMPT], start=True, stop=True)
            M.matmul(banks[:, 2 * s + 1, cut:TH], pool_w[:, g, :],
                     u_pad[:, g, POOL_AT[1]:POOL_AT[1] + L_SAMPLE], start=True, stop=True)\
                .then_inc(pool_ps, 1)
        pe.wait_ge(mix_ready, len(ATT_TILES) + 4)
        stage_blocks("w_out")
        ffn(1, "ffn2_0", norm_of("ffn2_0"))
        ffn(2, "ffn1_1", norm_of("ffn1_1"))

        im = norm_of("mix_1")
        nt = STAGE["tables"]
        pe.wait_ge(w_ready, nt + 1)
        pe.wait_ge(evac_done, nt)
        cd = pd = 0
        for kind, g in CD_ORDER:
            if kind == "cd":
                for i, (t0, rows, s) in enumerate(FT_TILES):
                    if cd >= 4:
                        pe.wait_ge(cd_done, cd - 3)
                    for kt in range(2):
                        if i == 0:
                            pe.wait_ge(xn_ready, im * KD + 2 * g + kt + 1)
                        x_pair = (xn_hi[:, 2 * g + kt, t0:t0 + rows], xn_lo[:, 2 * g + kt, t0:t0 + rows])
                        ins = triple(banks[0:rows, cd % 4, 0:DCOL], x_pair,
                                     (dft_hi[:, kt, :], dft_lo[:, kt, :]), kt == 0, kt == 1,
                                     (block_done, N_TABLE) if cd == kt == 0 else None)
                    ins.then_inc(cd_ps, 1)
                    cd += 1
                    if cd == 4:
                        statistics(im)
            else:
                parts = range(2) if kind == "pd" else range(1)
                for part in parts:
                    if pd == 0:
                        pe.wait_ge(w_ready, nt + N_TABLE)
                    if pd >= 4:
                        pe.wait_ge(pd_done, pd - 3)
                    if kind == "pd":
                        pe.wait_ge(cd_done, 8 * (g + 1))
                    else:
                        pe.wait_ge(yx_done, 16)
                    c0 = 0
                    for s in range(2):
                        tiles = [i for i, x_ in enumerate(FT_TILES) if x_[2] == s]
                        rows = FT[s][0]
                        for i in tiles:
                            if kind == "pd":
                                a, b = y_hi[0:rows, g % 2, i, part * P:(part + 1) * P], \
                                    y_lo[0:rows, g % 2, i, part * P:(part + 1) * P]
                                out = banks[:, 4 + pd % 4, c0:c0 + FOLD[s]]
                            else:
                                a, b = yx_hi[0:rows, i, :], yx_lo[0:rows, i, :]
                                out = banks[0:MX, 4 + pd % 4, c0:c0 + FOLD[s]]
                            at = cs_at(i, part)
                            ins = triple(out, (a, b), (cs_hi[0:rows, at:at + FOLD[s]],
                                                       cs_lo[0:rows, at:at + FOLD[s]]),
                                         i == tiles[0], i == tiles[-1])
                        c0 += FOLD[s]
                    ins.then_inc(pd_ps, 1)
                    pd += 1
        nf = STAGE["w_fourier"]
        pe.wait_ge(pd_done, pd)
        for m in range(KD):
            n = nf + m
            open_block(n % 2, n // 2)
            s = n % 2
            even, odd_ps = banks[:, 2 * s, 0:NF], banks[:, 2 * s + 1, 0:NF]
            for g in range(4):
                lhs = [w[s][:, g * P:(g + 1) * P] for w in (w_hi, w_lo)]
                triple(even, lhs, (xn_hi[:, 2 * g, 0:NF], xn_lo[:, 2 * g, 0:NF]), g == 0, False)
            lhs = [w[s][0:MX, 8 * P:9 * P] for w in (w_hi, w_lo)]
            triple(even, lhs, (px_hi[0:MX, :], px_lo[0:MX, :]), False, True)
            for g in range(4):
                lhs = [w[s][:, (4 + g) * P:(5 + g) * P] for w in (w_hi, w_lo)]
                ins = triple(odd_ps, lhs, (xn_hi[:, 2 * g + 1, 0:NF], xn_lo[:, 2 * g + 1, 0:NF]),
                             g == 0, g == 3)
            ins.then_inc(block_done, 1)
        ffn(3, "ffn2_1", norm_of("ffn2_1"))
        statistics(norm_of("final"))
        broadcast(norm_of("final"))

    ctx.close()


def alibi_table():
    r = np.arange(P)[:, None]
    j = np.arange(KEYS)[None, :] - P
    dist = np.abs(j - r)
    slopes = np.exp2(-8.0 * np.arange(1, N_HEADS + 1) / N_HEADS)
    table = np.where(dist[:, None, :] <= WINDOW, -slopes[None, :, None] * dist[:, None, :], NEG_INF)
    return table.astype(np.float32).reshape(P, N_HEADS * KEYS)


def edge_table():
    out = np.ones((4, 2, 2, PAD))
    for g, w in enumerate(POOL_WINDOWS):
        for s, (_, L) in enumerate(SEQS):
            t = np.arange(L)
            count = np.clip(t + w - w // 2, 0, L) - np.clip(t - w // 2, 0, L)
            out[g, s, 0], out[g, s, 1] = w / count[:PAD], w / count[-PAD:]
    return np.ascontiguousarray(np.broadcast_to(out.astype(np.float32).reshape(1, -1), (P, 4 * 4 * PAD)))


def dft_tables():
    out = np.zeros((N_TABLE, P, KMAX * P))
    n = np.arange(GROUP)[:, None]
    k = np.arange(P)[None, :]
    d = np.zeros((GROUP, DCOL))
    d[:, 0:P] = np.cos(2 * np.pi * (n * k % GROUP) / GROUP)
    d[:, P + 1:GROUP] = np.sin(2 * np.pi * (n * k[:, 1:] % GROUP) / GROUP)
    d[:, GROUP] = np.cos(np.pi * n[:, 0])
    out[0, :, 0:2 * DCOL] = d.reshape(2, P, DCOL).transpose(1, 0, 2).reshape(P, 2 * DCOL)
    cols = []
    for s, (rows, starts) in enumerate(FT):
        L = SEQS[s][1]
        norm = 1.0 / np.sqrt(GROUP * L)
        done = 0
        for t0 in starts:
            t = t0 + np.arange(rows)[:, None]
            angle = 2 * np.pi * ((t * np.arange(FOLD[s])[None, :]) % L) / L
            own = t >= done
            done = t0 + rows
            for f in (np.cos(angle), np.sin(angle)):
                f = np.where(own, f * norm, 0.0)
                f[np.abs(f) < 1e-14] = 0.0
                full = np.zeros((P, FOLD[s]))
                full[:rows] = f
                cols.append(full)
    cs = np.concatenate(cols, axis=1)
    for r, (a, b) in enumerate(((0, 4 * FOLD[0]), (4 * FOLD[0], 8 * FOLD[0]), (8 * FOLD[0], cs.shape[1]))):
        out[1 + r, :, 0:b - a] = cs[:, a:b]
    return out.astype(np.float32)


def kernel(**inputs):
    import concourse.bacc as bacc
    from concourse.bass_utils import run_bass_kernel_spmd

    a = {k: np.asarray(v) for k, v in inputs.items()}

    def columns(w, kt):
        lead = w.shape[:-2]
        w = w.reshape(*lead, kt, P, w.shape[-1] // P, P)
        n = len(lead)
        w = w.transpose(*range(n), n + 2, n + 1, n, n + 3)
        return w.reshape(*lead, w.shape[n], P, kt * P)

    tokens = np.concatenate([a["meta_tokens"], a["x_prompt"][0], a["meta_tokens"], a["x_sample"][0]])
    x = tokens.T.reshape(KD, P, T).transpose(1, 0, 2).reshape(P, KD * T)
    norms = [a["norm_ffn1"][0], a["norm_mix"][0], a["norm_ffn2"][0], a["norm_ffn1"][1],
             a["norm_mix"][1], a["norm_ffn2"][1], a["norm_final"], a["pool_scale"][0]]
    gains = np.concatenate(norms).reshape(-1, P).T
    sinks = np.broadcast_to(a["attn_sink"][0][None, :], (P, N_HEADS))
    gate_up, down = [], []
    for layer in range(2):
        for f in (1, 2):
            g = columns(a[f"ffn{f}_w_gate"][layer], KD)
            u = columns(a[f"ffn{f}_w_up"][layer], KD)
            gate_up.append(np.stack([g, u], axis=1).reshape(2 * FF_TILES, P, KD * P))
            down.append(columns(a[f"ffn{f}_w_down"][layer].reshape(2, HALF * P, D_MODEL), HALF)
                        .reshape(2 * KD, P, HALF * P))
    w = a["w_in_ap"][0]
    q = w[:, 0:512].reshape(D_MODEL, 2, 4, HEAD_DIM).transpose(0, 2, 1, 3).reshape(D_MODEL, 512)
    w_in = columns(np.concatenate([w[:, 768:], w[:, 640:768], w[:, 512:640], q], axis=1), KD)
    w_out = columns(a["w_out_ap"][0], KD)
    pool_w = a["pool_w"][0].transpose(1, 0, 2).reshape(P, 4 * P)
    wf = a["w_out_fourier"][0].reshape(4, GROUP, D_MODEL)
    low = wf[:, 0:P]
    high = np.concatenate([np.zeros((4, 1, D_MODEL), wf.dtype), wf[:, :P:-1]], axis=1)
    mid = np.concatenate([wf[:, P], np.zeros((P - 4, D_MODEL), wf.dtype)])
    w_fourier = columns(np.concatenate([low.reshape(4 * P, -1), high.reshape(4 * P, -1), mid]), FK)

    arrays = {
        "x": x, "gains": gains, "sinks": sinks, "ident_in": np.eye(P, dtype=np.float32),
        "alibi_in": alibi_table(), "edges_in": edge_table(), "pool_w_in": pool_w,
        "tables": dft_tables(), "gate_up": np.stack(gate_up), "down": np.stack(down), "w_in": w_in,
        "w_out": w_out, "w_fourier": w_fourier,
    }
    nc = bacc.Bacc("TRN2", target_bir_lowering=False, num_devices=1)
    launched, args = {}, []
    for name, value in arrays.items():
        value = np.ascontiguousarray(value)
        launched[name + "_dram"] = value
        args.append(nc.dram_tensor(name + "_dram", value.shape, mybir.dt.from_np(value.dtype),
                                   kind="ExternalInput").ap())
    args.append(nc.dram_tensor("y_dram", (P, KD * T), mybir.dt.float32, kind="ExternalOutput").ap())
    build(nc, *args)
    r = run_bass_kernel_spmd(nc, [launched], core_ids=[0])
    y = r.results[0]["y_dram"].reshape(P, KD, T).transpose(2, 1, 0).reshape(T, D_MODEL)
    return (np.ascontiguousarray(y[N_META:L_PROMPT])[None],
            np.ascontiguousarray(y[L_PROMPT + N_META:])[None])
```

```python
from contextlib import ExitStack

import numpy as np
import concourse.bass as bass
from concourse import mybir
from concourse.alu_op_type import AluOpType as ALU

P = 128
D_MODEL, D_FF, N_META = 1024, 2816, 16
L_PROMPT, L_SAMPLE = 512 + N_META, 256 + N_META
SEQS = ((0, L_PROMPT), (L_PROMPT, L_SAMPLE))
T = L_PROMPT + L_SAMPLE
TH = T // 2
KD = D_MODEL // P
FF_TILES = D_FF // P
HALF = FF_TILES // 2
KMAX = HALF
EPS = 1e-6
N_HEADS, HEAD_DIM, WINDOW = 8, 64, 128
POOL_WINDOWS = (2, 4, 8, 16)
NEG_INF = -1e30

PAD = 8
POOL_AT = (PAD, PAD + L_PROMPT + 2 * PAD)
POOL_W = T + 4 * PAD

ATT_TILES = [(s0, L, t, min(P, L - t)) for s0, L in SEQS for t in range(0, L, P)]
SCORES = 8
KEYS = 3 * P

FT = [(106, [0, 106, 212, 318, L_PROMPT - 106]), (92, [0, 92, L_SAMPLE - 92])]
FT_TILES = [(SEQS[s][0] + t, FT[s][0], s) for s in range(2) for t in FT[s][1]]
FOLD = [L // 2 + 2 for _, L in SEQS]
NF = sum(FOLD)
GROUP = 256
DCOL = GROUP + 2
MX = 66

NORMS = ("ffn1_0", "mix_0", "ffn2_0", "ffn1_1", "mix_1", "ffn2_1", "final")

FFN_BLOCKS = 2 * (2 * HALF + KD)
N_IN = 10
N_TABLE = 4
STAGE, _n = {}, 0
for _name, _count in (("ffn1_0", FFN_BLOCKS), ("w_in", N_IN), ("w_out", KD), ("ffn2_0", FFN_BLOCKS),
                      ("ffn1_1", FFN_BLOCKS), ("tables", N_TABLE), ("w_fourier", KD),
                      ("ffn2_1", FFN_BLOCKS)):
    STAGE[_name] = _n
    _n += _count
N_BLOCKS = _n
FK = 9


S0 = L_PROMPT
FFN_TOKENS = (
    (((0, 392),), ((392, 136), (S0 + N_META, 256))),
    (((0, TH),), ((TH, TH),)),
    (((0, TH),), ((TH, TH),)),
    (((N_META, 384),), ((N_META + 384, 128), (S0 + N_META, 256))),
)
FFN_COLS = [sum(n for _, n in bank_runs[0]) for bank_runs in FFN_TOKENS]
NORM_FFN = {"ffn1_0": 0, "ffn2_0": 1, "ffn1_1": 2, "ffn2_1": 3}


def runs_of(stage):
    f = NORM_FFN.get(stage)
    if f is None:
        return [(0, 0, T)]
    out, col = [], 0
    for t, n in (run for bank_runs in FFN_TOKENS[f] for run in bank_runs):
        if out and out[-1][0] + out[-1][2] == t:
            out[-1] = (out[-1][0], out[-1][1], out[-1][2] + n)
        else:
            out.append((t, col, n))
        col += n
    return out


def k_tiles(n):
    if n >= N_BLOCKS:
        return 0
    stage = max((s for s in STAGE if STAGE[s] <= n), key=lambda s: STAGE[s])
    at = n - STAGE[stage]
    if stage.startswith("ffn"):
        return KD if at % (2 * HALF + KD) < 2 * HALF else HALF
    return {"w_in": KD, "w_out": KD, "tables": KMAX, "w_fourier": FK}[stage]


def build(nc, x, gains, sinks, ident_in, alibi_in, edges_in, pool_w_in, tables, gate_up, down, w_in,
          w_out, w_fourier, y):
    f32, f32r = mybir.dt.float32, mybir.dt.float32r
    ACT = mybir.ActivationFunctionType
    ctx = ExitStack()

    def sb(name, shape, dt=f32):
        return ctx.enter_context(nc.sbuf_tensor(name, shape, dt))

    def scope(tensors):
        own = ExitStack()
        out = [own.enter_context(nc.sbuf_tensor(name, shape, dt)) for name, shape, dt in tensors]
        own.close()
        return out

    def sem(name):
        return ctx.enter_context(nc.semaphore(name))

    def as32(ap):
        return ap.bitcast(f32)

    h = sb("h", [P, KD, T])
    xn_hi = sb("xn_hi", [P, KD, T], f32r)
    xn_lo = sb("xn_lo", [P, KD, T], f32r)
    raw = [sb(f"raw{s}", [P, KMAX * P]) for s in range(2)]
    w_hi = [sb(f"w_hi{s}", [P, KMAX * P], f32r) for s in range(2)]
    w_lo = [sb(f"w_lo{s}", [P, KMAX * P], f32r) for s in range(2)]
    dft_hi = sb("dft_hi", [P, 2, DCOL], f32r)
    dft_lo = sb("dft_lo", [P, 2, DCOL], f32r)
    gain = sb("gain", [P, len(NORMS) * KD + 4])
    sink = sb("sink", [P, N_HEADS])
    ident = sb("ident", [P, P])
    ones = sb("ones", [P, P])
    minus_half = sb("minus_half", [P, KD])
    square = sb("square", [P, T])
    sum_sq = sb("sum_sq", [P, T])
    rstd = sb("rstd", [P, T])
    diag = sb("diag", [P, KD * 100])
    var = sb("var", [P, KD])
    rstd_tok = sb("rstd_tok", [P, KD])

    act_hi, act_lo, gate_t, up_t = scope([
        ("act_hi", [P, HALF * T], f32r), ("act_lo", [P, HALF * T], f32r),
        ("gate_t", [P, T], f32), ("up_t", [P, T], f32)])
    (q_sb, k_sb, v_sb, v_tok, u_pad, pool_a, pool_b, alibi, edges, pool_w, score, prob_t,
     row_max, neg_max, sink_d, row_sum, sink_e, rden) = scope([
        ("q_sb", [P, 4, T], f32), ("k_sb", [P, T], f32), ("v_sb", [P, T], f32),
        ("v_tok", [P, len(ATT_TILES), P], f32), ("u_pad", [P, 4, POOL_W], f32),
        ("pool_a", [P, POOL_W], f32), ("pool_b", [P, POOL_W], f32),
        ("alibi", [P, N_HEADS, KEYS], f32), ("edges", [P, 4, 2, 2, PAD], f32),
        ("pool_w", [P, 4, P], f32), ("score", [P, SCORES, KEYS], f32), ("prob_t", [P, 2, 3, 4, P], f32),
        ("row_max", [P, 2, 4], f32), ("neg_max", [P, 2, 4], f32), ("sink_d", [P, 2, 4], f32),
        ("row_sum", [P, 2, 4], f32), ("sink_e", [P, 2, 4], f32), ("rden", [P, 2, 4], f32)])
    (y_hi, y_lo, cs_hi, cs_lo, yx_hi, yx_lo, px_hi, px_lo, w_fold0, odd) = scope([
        ("y_hi", [P, 2, 8, DCOL], f32r), ("y_lo", [P, 2, 8, DCOL], f32r),
        ("cs_hi", [P, 2 * (5 * FOLD[0] + 3 * FOLD[1])], f32r),
        ("cs_lo", [P, 2 * (5 * FOLD[0] + 3 * FOLD[1])], f32r),
        ("yx_hi", [P, 8, MX], f32r), ("yx_lo", [P, 8, MX], f32r),
        ("px_hi", [P, NF], f32r), ("px_lo", [P, NF], f32r),
        ("w_fold0", [P, 8 * P], f32), ("odd", [P, NF], f32)])
    w_fold1, = scope([("w_fold1", [P, 8 * P], f32)])
    w_fold = (w_fold0, w_fold1)

    banks = ctx.enter_context(nc.psum_tensor("banks", [P, 8, 512], f32))
    AUX, STAT = 4, 6

    def slot(s, cols=TH):
        return banks[:, 2 * s:2 * s + 2, 0:cols]

    def two(ap):
        return ap.rearrange("p (b t) -> p b t", b=2)

    const_in = sem("const_in")
    h_in = [sem(f"h_in{k}") for k in range(KD)]
    mix_in = sem("mix_in")
    raw_full = [sem(f"raw_full{s}") for s in range(2)]
    w_hi_done = sem("w_hi_done")
    w_ready = sem("w_ready")
    fold_done = sem("fold_done")
    block_done = sem("block_done")
    evac_done = sem("evac_done")
    silu_done = sem("silu_done")
    prod_done = sem("prod_done")
    act_hi_done = sem("act_hi_done")
    act_ready = sem("act_ready")
    sq_done = sem("sq_done")
    xn_hi_done = sem("xn_hi_done")
    xn_ready = sem("xn_ready")
    sum_done = sem("sum_done")
    setup_done = sem("setup_done")
    stat_done = sem("stat_done")
    var_done = sem("var_done")
    rstd_tok_done = sem("rstd_tok_done")
    diag_done = sem("diag_done")
    bcast_done = sem("bcast_done")
    rstd_done = sem("rstd_done")
    y_done = sem("y_done")
    y_out = sem("y_out")

    block = ctx.enter_context(nc.Block())

    def norm_of(stage):
        return NORMS.index(stage)

    LATE_NORMS = (norm_of("ffn2_0"), norm_of("ffn2_1"))
    BCAST_NORMS = [0, 1, 2, 3, 5, 6]

    @block.sync
    def _(sp):
        def load(slot_no, n_half, source, cols, wait=True, first=False):
            if not first:
                sp.wait_ge(w_ready, n_half * 2 + slot_no - 1)
            sp.dma_start(raw[slot_no][:, 0:cols], source).then_inc(raw_full[slot_no], 16)

        def load_ffn(f, n0):
            for half in range(2):
                g0 = half * 2 * HALF
                start = n0 + half * (2 * HALF + KD)
                lo = 0
                if start == 0:
                    for s in range(2):
                        load(s, 0, gate_up[f, s], KD * P, first=True)
                    lo = 1
                with nc.sync.Fori(lo, HALF) as i:
                    for s in range(2):
                        load(s, i + start // 2, gate_up[f, bass.ds(i * 2 + (g0 + s), 1)]
                             .rearrange("o p c -> (o p) c"), KD * P)
                start += 2 * HALF
                with nc.sync.Fori(0, KD // 2) as i:
                    for s in range(2):
                        load(s, i + start // 2, down[f, bass.ds(i * 2 + (half * KD + s), 1)]
                             .rearrange("o p c -> (o p) c"), HALF * P)

        def load_stage(stage, source, cols):
            start = STAGE[stage]
            with nc.sync.Fori(0, source.shape[0] // 2) as i:
                for s in range(2):
                    load(s, i + start // 2, source[bass.ds(i * 2 + s, 1)]
                         .rearrange("o p c -> (o p) c"), cols)

        load_ffn(0, STAGE["ffn1_0"])
        load_stage("w_in", w_in, KD * P)
        sp.wait_ge(block_done, STAGE["w_in"])
        for dst, src in ((alibi, alibi_in), (edges, edges_in), (pool_w, pool_w_in)):
            sp.dma_start(dst[:].rearrange("p a b -> p (a b)") if len(dst.shape) == 3 else
                         dst[:].rearrange("p a b c d -> p (a b c d)"), src[:, :]).then_inc(mix_in, 16)
        load_stage("w_out", w_out, KD * P)
        load_ffn(1, STAGE["ffn2_0"])
        load_ffn(2, STAGE["ffn1_1"])
        load_stage("tables", tables, KMAX * P)
        load_stage("w_fourier", w_fourier, FK * P)
        load_ffn(3, STAGE["ffn2_1"])
        for k in range(KD):
            sp.wait_ge(y_done, k + 1)
            sp.dma_start(y[:, k * T:(k + 1) * T], h[:, k, :]).then_inc(y_out, 16)
        sp.wait_ge(y_out, 16 * KD)

    pad_done = sem("pad_done")
    pooled_done = sem("pooled_done")
    pool_chain = sem("pool_chain")
    v_tok_ps = sem("v_tok_ps")
    v_tok_done = sem("v_tok_done")
    score_ps = sem("score_ps")
    score_done = sem("score_done")
    neg_done = sem("neg_done")
    sinkd_done = sem("sinkd_done")
    prob_done = sem("prob_done")
    sink_e_done = sem("sink_e_done")
    prob_t_ps = sem("prob_t_ps")
    prob_t_done = sem("prob_t_done")
    den_done = sem("den_done")
    rden_done = sem("rden_done")
    norm_done = sem("norm_done")
    quad_out = sem("quad_out")
    mix_hi_done = sem("mix_hi_done")
    mix_ready = sem("mix_ready")
    pool_ps = sem("pool_ps")
    yx_zero = sem("yx_zero")
    cd_ps = sem("cd_ps")
    cd_hi = sem("cd_hi")
    cd_done = sem("cd_done")
    yx_done = sem("yx_done")
    pd_ps = sem("pd_ps")
    pd_hi = sem("pd_hi")
    pd_done = sem("pd_done")
    odd_done = sem("odd_done")
    odd_added = sem("odd_added")
    odd_sample = sem("odd_sample")

    CD_ORDER = [("cd", 0), ("cd", 1), ("pd", 0), ("cd", 2), ("pd", 1), ("cd", 3), ("pd", 2),
                ("pd", 3), ("px", 4)]

    TABLE_COLS = {1: (0, 4 * FOLD[0]), 2: (4 * FOLD[0], 8 * FOLD[0]),
                  3: (8 * FOLD[0], 10 * FOLD[0] + 6 * FOLD[1])}

    FIRST_CD = (0, 1, 2, 3, 4, 5, 7)

    def cd_bank(cd):
        return FIRST_CD[cd] if cd < len(FIRST_CD) else cd % 4

    def cs_at(tile, part):
        if tile < 5:
            return (2 * tile + part) * FOLD[0]
        return 10 * FOLD[0] + (2 * (tile - 5) + part) * FOLD[1]

    UNITS = [(i, hd) for i in range(len(ATT_TILES)) for hd in range(N_HEADS)]

    def keys_of(i):
        s0, L, t, rows = ATT_TILES[i]
        return max(0, t - P), min(L, t + 2 * P)

    @block.gpsimd
    def _(pool):
        nc.gpsimd.memset(ones[:, :], 1.0).then_inc(setup_done, 1)
        nc.gpsimd.memset(minus_half[:, :], -0.5).then_inc(setup_done, 1)
        pool.wait_ge(setup_done, 2)

        def power(i):
            pool.wait_ge(var_done, i + 1)
            if i == norm_of("mix_1"):
                for s, (rows, at) in enumerate(FT):
                    c = slice(0, 5) if s == 0 else slice(5, 8)
                    last = nc.gpsimd.tensor_tensor(rstd_tok[0:rows, c], var[0:rows, c],
                                                   minus_half[0:rows, c], ALU.pow)
            else:
                last = nc.gpsimd.tensor_tensor(rstd_tok[0:100, :], var[0:100, :],
                                               minus_half[0:100, :], ALU.pow)
            last.then_inc(rstd_tok_done, 1)

        chain = [0]

        def then(ins):
            chain[0] += 1
            ins.then_inc(pool_chain, 1)
            pool.wait_ge(pool_chain, chain[0])

        power(norm_of("ffn1_0"))
        pool.wait_ge(block_done, STAGE["w_in"])
        for a, b in ((0, PAD), (PAD + L_PROMPT, POOL_AT[1]), (POOL_AT[1] + L_SAMPLE, POOL_W)):
            nc.gpsimd.memset(u_pad[:, :, a:b], 0.0).then_inc(pad_done, 1)
        power(norm_of("mix_0"))
        pool.wait_ge(mix_in, 48)
        for g, w in enumerate(POOL_WINDOWS):
            pool.wait_ge(pad_done, 3)
            pool.wait_ge(evac_done, STAGE["w_in"] + g + 1)
            u = u_pad[:, g, :]
            lo, hi = 1, POOL_W
            then(nc.gpsimd.tensor_tensor(pool_a[:, lo:hi], u[:, lo - 1:hi - 1], u[:, lo:hi], ALU.add))
            src, dst, size = pool_a, pool_b, 2
            while size < w:
                q = size // 2
                then(nc.gpsimd.tensor_tensor(dst[:, lo + q:hi - q], src[:, lo:hi - 2 * q],
                                             src[:, lo + 2 * q:hi], ALU.add))
                lo, hi, size = lo + q, hi - q, 2 * size
                src, dst = dst, src
            ends = (POOL_AT[0] + L_PROMPT - PAD, POOL_AT[1] + L_SAMPLE - PAD)
            for side, (a, b) in enumerate((POOL_AT, ends)):
                part = src[:, a:b + PAD].rearrange("p c -> p c")
                for s, at in enumerate((a, b)):
                    last = nc.gpsimd.tensor_tensor(src[:, at:at + PAD], src[:, at:at + PAD],
                                                   edges[:, g, s, side, :], ALU.mult)
                    if not (side and s):
                        last.then_inc(pool_chain, 1)
                        chain[0] += 1
            then(last)
            a, b = POOL_AT[0], POOL_AT[1] + L_SAMPLE
            then(nc.gpsimd.tensor_scalar(dst[:, a:b], src[:, a:b], 1.0 / w, None, ALU.mult))
            nc.gpsimd.tensor_tensor(u[:, a:b], dst[:, a:b], u[:, a:b], ALU.subtract)\
                .then_inc(pooled_done, 1)
            pool.wait_ge(pooled_done, g + 1)
        power(norm_of("ffn2_0"))
        power(norm_of("ffn1_1"))
        pool.wait_ge(block_done, STAGE["tables"])
        nc.gpsimd.memset(as32(yx_hi[:, :, :]), 0.0).then_inc(yx_zero, 1)
        nc.gpsimd.memset(as32(yx_lo[:, :, :]), 0.0).then_inc(yx_zero, 1)
        power(norm_of("mix_1"))
        pool.wait_ge(yx_zero, 2)

        nf = STAGE["w_fourier"]

        def fold(n):
            pool.wait_ge(raw_full[n % 2], 16 * (n // 2 + 1))
            if n == nf + 1:
                pool.wait_ge(pd_ps, 9)
            elif n > nf + 1:
                pool.wait_ge(w_ready, n - 1)
            a, b = raw[n % 2][:, 0:4 * P], raw[n % 2][:, 4 * P:8 * P]
            out = w_fold[(n - nf) % 2]
            nc.gpsimd.tensor_tensor(out[:, 0:4 * P], a, b, ALU.add).then_inc(fold_done, 1)
            nc.gpsimd.tensor_tensor(out[:, 4 * P:8 * P], b, a, ALU.subtract).then_inc(fold_done, 1)

        cd = 0
        for kind, g in CD_ORDER:
            if kind == "cd":
                cd += 1
                pool.wait_ge(cd_done, 8 * cd)
                for (dst, src) in ((yx_hi, y_hi), (yx_lo, y_lo)):
                    for s, (rows, _) in enumerate(FT):
                        c = slice(0, 5) if s == 0 else slice(5, 8)
                        last = nc.gpsimd.tensor_copy(dst[0:rows, c, g:g + 1],
                                                     src[0:rows, g % 2, c, GROUP:GROUP + 1])
                        last.then_inc(yx_done, 1)
        for n in (nf, nf + 1):
            fold(n)
        for m in range(KD):
            if m + 2 < KD:
                fold(nf + m + 2)
            pool.wait_ge(odd_done, m + 1)
            half = L_PROMPT // 2 + 1
            fwd, bwd = h[:, m, 0:half], h[:, m, half:L_PROMPT]
            nc.gpsimd.tensor_tensor(fwd, fwd, odd[:, 0:half], ALU.add).then_inc(odd_added, 1)
            nc.gpsimd.tensor_tensor(bwd, bwd, odd[:, half - 2:0:-1], ALU.subtract)\
                .then_inc(odd_added, 1)
        power(norm_of("ffn2_1"))
        power(norm_of("final"))

    @block.scalar
    def _(act):
        A = nc.scalar

        def split_hi(s, n, n_half, k, first=False):
            act.wait_ge(raw_full[s], (n_half + 1) * 16)
            if not first:
                act.wait_ge(block_done, n_half * 2 + s - 1)
            A.activation(w_hi[s][:, 0:k * P], raw[s][:, 0:k * P], ACT.Copy).then_inc(w_hi_done, 1)

        def split_hi_static(n):
            if n >= N_BLOCKS:
                return
            s, stage_t, stage_f = n % 2, STAGE["tables"], STAGE["w_fourier"]
            if stage_t <= n < stage_f:
                act.wait_ge(raw_full[s], 16 * (n // 2 + 1))
                r = n - stage_t
                if r:
                    act.wait_ge(block_done, stage_t)
                if r == 0:
                    A.activation(dft_hi[:, :, :], raw[s][:, 0:2 * DCOL].rearrange("p (a b) -> p a b", a=2),
                                 ACT.Copy).then_inc(w_hi_done, 1)
                else:
                    a, b = TABLE_COLS[r]
                    rows = FT[0][0]
                    A.activation(cs_hi[0:rows, a:b], raw[s][0:rows, 0:b - a], ACT.Copy)\
                        .then_inc(w_hi_done, 1)
            elif stage_f <= n < stage_f + KD:
                act.wait_ge(block_done, n - 1)
                act.wait_ge(fold_done, 2 * (n - stage_f) + 2)
                A.activation(w_hi[s][:, 0:8 * P], w_fold[(n - stage_f) % 2][:, :], ACT.Copy)
                A.activation(w_hi[s][:, 8 * P:9 * P], raw[s][:, 8 * P:9 * P], ACT.Copy)\
                    .then_inc(w_hi_done, 1)
            else:
                split_hi(s, n, n // 2, k_tiles(n), first=n < 2)

        def gain_hi(i, m):
            for t, c, n in runs_of(NORMS[i]):
                last = A.activation(xn_hi[:, m, c:c + n], h[:, m, t:t + n], ACT.Copy,
                                    scale=gain[:, i * KD + m:i * KD + m + 1])
            last.then_inc(xn_hi_done, 1)

        def norm_hi(i, m):
            if i < len(NORMS) - 1 and i not in LATE_NORMS:
                gain_hi(i, m)
            act.wait_ge(sum_done, 9 * i + m + 1)
            A.activation(square[:, :], h[:, m, :], ACT.Square).then_inc(sq_done, 1)

        def ffn(f, stage, norm_after):
            n0, W = STAGE[stage], 2 * FFN_COLS[f]
            j0 = f * FF_TILES
            for half in range(2):
                b0 = n0 + half * (2 * HALF + KD)
                jj = j0 + half * HALF

                def pair(i, nxt):
                    act.wait_ge(block_done, i * 2 + (b0 + 1))
                    nxt(0)
                    act.wait_ge(evac_done, i * 2 + (b0 + 1))
                    A.activation(gate_t[:, 0:W], gate_t[:, 0:W], ACT.Silu).then_inc(silu_done, 1)
                    act.wait_ge(block_done, i * 2 + (b0 + 2))
                    nxt(1)
                    act.wait_ge(prod_done, i + (jj + 1))
                    A.activation(act_hi[:, bass.ds(i * T, W)], up_t[:, 0:W], ACT.Copy)\
                        .then_inc(act_hi_done, 1)

                with A.Fori(0, HALF - 1) as i:
                    pair(i, lambda s: split_hi(s, None, i + (b0 // 2 + 1), KD))
                last = b0 + 2 * (HALF - 1)
                pair(HALF - 1, lambda s: split_hi_static(last + 2 + s))
                d0 = b0 + 2 * HALF
                for m in range(KD):
                    act.wait_ge(block_done, d0 + m + 1)
                    split_hi_static(d0 + m + 2)
                    if half:
                        act.wait_ge(evac_done, d0 + m + 1)
                        norm_hi(norm_after, m)

        for k in range(KD):
            act.dma_start(h[:, k, :], x[:, k * T:(k + 1) * T]).then_inc(h_in[k], 16)
            if k == 0:
                for dst, src in ((gain, gains), (sink, sinks), (ident, ident_in)):
                    act.dma_start(dst[:, :], src[:, :]).then_inc(const_in, 16)
        split_hi_static(0)
        act.wait_ge(const_in, 48)
        for m in range(KD):
            act.wait_ge(h_in[m], 16)
            norm_hi(0, m)
            if m == 0:
                split_hi_static(1)
        ffn(0, "ffn1_0", norm_of("mix_0"))

        b0 = STAGE["w_in"]
        for r in range(N_IN):
            act.wait_ge(block_done, b0 + r + 1)
            split_hi_static(b0 + r + 2)
        for i, (s0, L, t, rows) in enumerate(ATT_TILES):
            act.wait_ge(v_tok_ps, i + 1)
            A.activation(v_tok[0:rows, i, :], banks[0:rows, 6 + i % 2, 0:P], ACT.Copy)\
                .then_inc(v_tok_done, 1)

        def exp_quad(q):
            i = q // 2
            rows = ATT_TILES[i][3]
            k0, k1 = keys_of(i)
            act.wait_ge(neg_done, q + 1)
            for c in range(4):
                u = 4 * q + c
                A.activation(score[0:rows, u % SCORES, 0:k1 - k0],
                             score[0:rows, u % SCORES, 0:k1 - k0],
                             ACT.Exp, bias=neg_max[0:rows, q % 2, c:c + 1],
                             accum_out=row_sum[0:rows, q % 2, c:c + 1]).then_inc(prob_done, 1)
            act.wait_ge(sinkd_done, q + 1)
            A.activation(sink_e[0:rows, q % 2, :], sink_d[0:rows, q % 2, :], ACT.Exp)\
                .then_inc(sink_e_done, 1)

        def prob_copy(u):
            i = u // 8
            rows = ATT_TILES[i][3]
            k0, k1 = keys_of(i)
            q, c = divmod(u, 4)
            act.wait_ge(prob_t_ps, u + 1)
            if c == 0 and q >= 2:
                act.wait_ge(quad_out, q - 1)
            full, kr = divmod(k1 - k0, P)
            if kr:
                A.activation(prob_t[0:kr, q % 2, full, c, 0:rows],
                             banks[0:kr, 3 + u % 2, full * P:full * P + rows], ACT.Copy)\
                    .then_inc(prob_t_done, 1)
            A.activation(prob_t[:, q % 2, 0:full, c, 0:rows],
                         banks[:, 3 + u % 2, 0:full * P].rearrange("p (j r) -> p j r", r=P)[:, :, 0:rows],
                         ACT.Copy).then_inc(prob_t_done, 1)

        def out_hi(i):
            s0, L, t, rows = ATT_TILES[i]
            act.wait_ge(quad_out, 2 * i + 2)
            A.activation(xn_hi[:, 0:4, s0 + t:s0 + t + rows],
                         banks[:, 5 + i % 3, :].rearrange("p (k r) -> p k r", k=4)[:, :, 0:rows],
                         ACT.Copy).then_inc(mix_hi_done, 1)

        NQ = len(ATT_TILES) * 2
        for q in range(NQ + 1):
            if q < NQ:
                exp_quad(q)
            if q >= 1:
                for c in range(4):
                    prob_copy(4 * (q - 1) + c)
                if q >= 4 and q % 2 == 0:
                    out_hi((q - 4) // 2)
        out_hi(len(ATT_TILES) - 1)
        for g in range(4):
            act.wait_ge(pool_ps, g + 1)
            sc = gain[:, len(NORMS) * KD + g:len(NORMS) * KD + g + 1]
            A.activation(two(xn_hi[:, 4 + g, :]), slot(g % 2), ACT.Copy, scale=sc)\
                .then_inc(mix_hi_done, 1)
        b0 = STAGE["w_out"]
        for m in range(KD):
            act.wait_ge(block_done, b0 + m + 1)
            split_hi_static(b0 + m + 2)
            act.wait_ge(evac_done, b0 + m + 1)
            norm_hi(norm_of("ffn2_0"), m)
        for m in range(KD):
            gain_hi(norm_of("ffn2_0"), m)
        ffn(1, "ffn2_0", norm_of("ffn1_1"))
        ffn(2, "ffn1_1", norm_of("mix_1"))

        nt = STAGE["tables"]
        split_hi_static(nt + 2)
        split_hi_static(nt + 3)
        act.wait_ge(rstd_tok_done, norm_of("mix_1") + 1)
        cd = pd = 0
        for kind, g in CD_ORDER:
            if kind == "cd":
                for i, (t0, rows, s) in enumerate(FT_TILES):
                    act.wait_ge(cd_ps, cd + 1)
                    if g >= 2 and i == 0:
                        act.wait_ge(yx_done, 4 * (g - 1))
                    A.activation(y_hi[0:rows, g % 2, i, :], banks[0:rows, cd_bank(cd), 0:DCOL], ACT.Copy,
                                 scale=rstd_tok[0:rows, i:i + 1]).then_inc(cd_hi, 1)
                    cd += 1
            elif kind == "pd":
                for part in range(2):
                    act.wait_ge(pd_ps, pd + 1)
                    A.activation(xn_hi[:, 2 * g + part, 0:NF], banks[:, 4 + pd % 4, 0:NF], ACT.Copy)\
                        .then_inc(pd_hi, 1)
                    pd += 1
            else:
                act.wait_ge(pd_ps, pd + 1)
                A.activation(px_hi[0:MX, :], banks[0:MX, 4 + pd % 4, 0:NF], ACT.Copy)\
                    .then_inc(pd_hi, 1)
        nf = STAGE["w_fourier"]
        split_hi_static(nf)
        split_hi_static(nf + 1)
        for m in range(KD):
            act.wait_ge(block_done, nf + m + 1)
            if m:
                act.wait_ge(odd_added, 2 * m)
                act.wait_ge(odd_sample, m)
            A.activation(odd[:, :], banks[:, 2 * (m % 2) + 1, 0:NF], ACT.Copy).then_inc(odd_done, 1)
            split_hi_static(nf + m + 2)
            act.wait_ge(evac_done, nf + m + 1)
            norm_hi(norm_of("ffn2_1"), m)
        for m in range(KD):
            gain_hi(norm_of("ffn2_1"), m)
        ffn(3, "ffn2_1", norm_of("final"))

    @block.vector
    def _(dve):
        V = nc.vector

        def split_lo(s, n_half, k):
            dve.wait_ge(w_hi_done, n_half * 2 + (s + 1))
            V.tensor_tensor(w_lo[s][:, 0:k * P], raw[s][:, 0:k * P], as32(w_hi[s][:, 0:k * P]),
                            ALU.subtract).then_inc(w_ready, 1)

        def split_lo_static(n):
            if n >= N_BLOCKS:
                return
            s, stage_t, stage_f = n % 2, STAGE["tables"], STAGE["w_fourier"]
            if stage_t <= n < stage_f:
                dve.wait_ge(w_hi_done, n + 1)
                r = n - stage_t
                if r == 0:
                    V.tensor_tensor(dft_lo[:, :, :], raw[s][:, 0:2 * DCOL].rearrange("p (a b) -> p a b", a=2),
                                    as32(dft_hi[:, :, :]), ALU.subtract).then_inc(w_ready, 1)
                else:
                    a, b = TABLE_COLS[r]
                    rows = FT[0][0]
                    V.tensor_tensor(cs_lo[0:rows, a:b], raw[s][0:rows, 0:b - a],
                                    as32(cs_hi[0:rows, a:b]), ALU.subtract).then_inc(w_ready, 1)
            elif stage_f <= n < stage_f + KD:
                dve.wait_ge(w_hi_done, n + 1)
                V.tensor_tensor(w_lo[s][:, 0:8 * P], w_fold[(n - stage_f) % 2][:, :], as32(w_hi[s][:, 0:8 * P]),
                                ALU.subtract)
                V.tensor_tensor(w_lo[s][:, 8 * P:9 * P], raw[s][:, 8 * P:9 * P],
                                as32(w_hi[s][:, 8 * P:9 * P]), ALU.subtract).then_inc(w_ready, 1)
            else:
                split_lo(s, n // 2, k_tiles(n))

        def gain_lo(i, m):
            dve.wait_ge(xn_hi_done, i * KD + m + 1)
            for t, c, n in runs_of(NORMS[i]):
                last = V.scalar_tensor_tensor(xn_lo[:, m, c:c + n], h[:, m, t:t + n],
                                              gain[:, i * KD + m:i * KD + m + 1],
                                              as32(xn_hi[:, m, c:c + n]), ALU.mult, ALU.subtract)
            last.then_inc(xn_ready, 1)

        def norm_lo(i, m):
            if i < len(NORMS) - 1 and i not in LATE_NORMS:
                gain_lo(i, m)
            dve.wait_ge(sq_done, i * KD + m + 1)
            dve.wait_ge(sum_done, 9 * i + m + 1)
            V.tensor_tensor(sum_sq[:, :], sum_sq[:, :], square[:, :], ALU.add).then_inc(sum_done, 1)

        def variance(i):
            dve.wait_ge(stat_done, i + 1)
            if i == norm_of("mix_1"):
                for s, (rows, at) in enumerate(FT):
                    c = slice(0, 5) if s == 0 else slice(5, 8)
                    last = V.tensor_scalar(var[0:rows, c], banks[0:rows, STAT, c], 1.0 / D_MODEL,
                                           EPS, ALU.mult, ALU.add)
                    if s == 0:
                        last.then_inc(evac_done, N_TABLE)
            else:
                last = V.tensor_scalar(var[0:100, :], banks[0:100, STAT, 0:KD], 1.0 / D_MODEL, EPS,
                                       ALU.mult, ALU.add)
            last.then_inc(var_done, 1)
            if i < len(NORMS) - 1:
                V.memset(sum_sq[:, :], 0.0).then_inc(sum_done, 1)

        def diagonal(i):
            dve.wait_ge(rstd_tok_done, i + 1)
            V.tensor_tensor(diag[0:100, :].rearrange("p (k t) -> p k t", k=KD),
                            ident[0:100, None, 0:100].to_broadcast([100, KD, 100]),
                            rstd_tok[0:100, :, None].to_broadcast([100, KD, 100]),
                            ALU.mult).then_inc(diag_done, 1)

        def spread(i):
            b = BCAST_NORMS.index(i) + 1
            if i not in LATE_NORMS:
                diagonal(i)
            dve.wait_ge(bcast_done, b)
            cols = FFN_COLS[NORM_FFN[NORMS[i]]] if NORMS[i] in NORM_FFN else TH
            V.tensor_copy(two(rstd[:, 0:2 * cols]), banks[:, AUX:AUX + 2, 0:cols])\
                .then_inc(rstd_done, 1)
            dve.wait_ge(rstd_done, b)

        def ffn(f, stage, norm_after, norm_before):
            n0, C = STAGE[stage], FFN_COLS[f]
            W = 2 * C
            j0 = f * FF_TILES
            for half in range(2):
                b0 = n0 + half * (2 * HALF + KD)
                jj = j0 + half * HALF

                def pair(i, nxt):
                    dve.wait_ge(block_done, i * 2 + (b0 + 1))
                    V.tensor_tensor(two(gate_t[:, 0:W]), slot(0, C), two(rstd[:, 0:W]), ALU.mult)\
                        .then_inc(evac_done, 1)
                    nxt(0)
                    dve.wait_ge(block_done, i * 2 + (b0 + 2))
                    dve.wait_ge(evac_done, i * 2 + (b0 + 1))
                    V.tensor_tensor(two(up_t[:, 0:W]), slot(1, C), two(rstd[:, 0:W]), ALU.mult)\
                        .then_inc(evac_done, 1)
                    dve.wait_ge(silu_done, i + (jj + 1))
                    dve.wait_ge(evac_done, i * 2 + (b0 + 2))
                    V.tensor_tensor(up_t[:, 0:W], up_t[:, 0:W], gate_t[:, 0:W], ALU.mult)\
                        .then_inc(prod_done, 1)
                    nxt(1)
                    dve.wait_ge(act_hi_done, i + (jj + 1))
                    V.tensor_tensor(act_lo[:, bass.ds(i * T, W)], up_t[:, 0:W],
                                    as32(act_hi[:, bass.ds(i * T, W)]), ALU.subtract)\
                        .then_inc(act_ready, 1)

                if half == 0:
                    variance(norm_before)
                    for m in range(KD if norm_before in LATE_NORMS else 0):
                        if m == 2:
                            diagonal(norm_before)
                        gain_lo(norm_before, m)
                    spread(norm_before)
                with V.Fori(0, HALF - 1) as i:
                    pair(i, lambda s: split_lo(s, i + (b0 // 2 + 1), KD))
                last = b0 + 2 * (HALF - 1)
                pair(HALF - 1, lambda s: split_lo_static(last + 2 + s))
                d0 = b0 + 2 * HALF
                for m in range(KD):
                    dve.wait_ge(block_done, d0 + m + 1)
                    add_to_h(f, m).then_inc(evac_done, 1)
                    if half:
                        norm_lo(norm_after, m)
                    split_lo_static(d0 + m + 2)

        def add_to_h(f, m):
            if len(FFN_TOKENS[f][1]) == 1:
                return V.scalar_tensor_tensor(two(h[:, m, :]), slot(m % 2), 0.5, two(h[:, m, :]),
                                              ALU.mult, ALU.add)
            parts = []
            for b, bank_runs in enumerate(FFN_TOKENS[f]):
                c = 0
                for t, n in bank_runs:
                    parts.append((t, b, c, n))
                    c += n
            if f == 0:
                parts.append((S0, 0, 0, N_META))
            for t, b, c, n in parts:
                last = V.scalar_tensor_tensor(h[:, m, t:t + n], banks[:, 2 * (m % 2) + b, c:c + n],
                                              0.5, h[:, m, t:t + n], ALU.mult, ALU.add)
            return last

        V.memset(sum_sq[:, :], 0.0).then_inc(sum_done, 1)
        split_lo_static(0)
        dve.wait_ge(const_in, 48)
        for m in range(KD):
            dve.wait_ge(h_in[m], 16)
            norm_lo(0, m)
            if m == 0:
                split_lo_static(1)
        ffn(0, "ffn1_0", norm_of("mix_0"), norm_of("ffn1_0"))

        b0 = STAGE["w_in"]
        variance(norm_of("mix_0"))
        spread(norm_of("mix_0"))
        for r in range(N_IN):
            s = r % 2
            dve.wait_ge(block_done, b0 + r + 1)
            if r < 4:
                cut = L_PROMPT - TH
                V.tensor_tensor(u_pad[:, r, PAD:PAD + TH], banks[:, 2 * s, 0:TH], rstd[:, 0:TH],
                                ALU.mult)
                V.tensor_tensor(u_pad[:, r, PAD + TH:PAD + L_PROMPT], banks[:, 2 * s + 1, 0:cut],
                                rstd[:, TH:L_PROMPT], ALU.mult)
                V.tensor_tensor(u_pad[:, r, POOL_AT[1]:POOL_AT[1] + L_SAMPLE],
                                banks[:, 2 * s + 1, cut:TH], rstd[:, L_PROMPT:T],
                                ALU.mult).then_inc(evac_done, 1)
            elif r < 6:
                dst = v_sb if r == 4 else k_sb
                V.tensor_tensor(two(dst[:, :]), slot(s), two(rstd[:, :]), ALU.mult)\
                    .then_inc(evac_done, 1)
            else:
                V.scalar_tensor_tensor(two(q_sb[:, r - 6, :]), slot(s), HEAD_DIM ** -0.5,
                                       two(rstd[:, :]), ALU.mult, ALU.mult).then_inc(evac_done, 1)
            split_lo_static(b0 + r + 2)
        dve.wait_ge(mix_in, 48)

        def score_quad(q):
            i = q // 2
            rows = ATT_TILES[i][3]
            k0, k1 = keys_of(i)
            off = k0 - (ATT_TILES[i][2] - P)
            for c in range(4):
                u = 4 * q + c
                hd = u % 8
                if c == 3 and q:
                    norm_quad(q - 1)
                dve.wait_ge(score_ps, u + 1)
                if u >= SCORES:
                    dve.wait_ge(prob_t_ps, u - SCORES + 1)
                V.tensor_tensor_reduce(out=score[0:rows, u % SCORES, 0:k1 - k0],
                                       in0=banks[0:rows, u % 3, 0:k1 - k0],
                                       in1=alibi[0:rows, hd, off:off + k1 - k0], scale=1.0,
                                       scalar=sink[0:rows, hd:hd + 1], op0=ALU.add, op1=ALU.max,
                                       accum_out=row_max[0:rows, q % 2, c:c + 1])\
                    .then_inc(score_done, 1)
            dve.wait_ge(score_done, 4 * q + 4)
            if q >= 2:
                dve.wait_ge(sink_e_done, q - 1)
            V.tensor_scalar(neg_max[0:rows, q % 2, :], row_max[0:rows, q % 2, :], -1.0, None,
                            ALU.mult).then_inc(neg_done, 1)
            dve.wait_ge(neg_done, q + 1)
            hb = 4 * (q % 2)
            V.tensor_tensor(sink_d[0:rows, q % 2, :], sink[0:rows, hb:hb + 4],
                            neg_max[0:rows, q % 2, :], ALU.add).then_inc(sinkd_done, 1)

        def norm_quad(q):
            i = q // 2
            rows = ATT_TILES[i][3]
            k0, k1 = keys_of(i)
            dve.wait_ge(prob_done, 4 * q + 4)
            dve.wait_ge(sink_e_done, q + 1)
            V.tensor_tensor(rden[0:rows, q % 2, :], row_sum[0:rows, q % 2, :],
                            sink_e[0:rows, q % 2, :], ALU.add).then_inc(den_done, 1)
            dve.wait_ge(den_done, q + 1)
            V.reciprocal(rden[0:rows, q % 2, :], rden[0:rows, q % 2, :]).then_inc(rden_done, 1)
            dve.wait_ge(rden_done, q + 1)
            for c in range(4):
                at = score[0:rows, (4 * q + c) % SCORES, 0:k1 - k0]
                V.tensor_scalar(at, at, rden[0:rows, q % 2, c:c + 1], None, ALU.mult)\
                    .then_inc(norm_done, 1)

        def tile_lo(i):
            s0, L, t, rows = ATT_TILES[i]
            dve.wait_ge(mix_hi_done, i + 1)
            V.tensor_tensor(xn_lo[:, 0:4, s0 + t:s0 + t + rows],
                            banks[:, 5 + i % 3, :].rearrange("p (k r) -> p k r", k=4)[:, :, 0:rows],
                            as32(xn_hi[:, 0:4, s0 + t:s0 + t + rows]),
                            ALU.subtract).then_inc(mix_ready, 1)

        NQ = len(ATT_TILES) * 2
        for q in range(NQ):
            score_quad(q)
            if q >= 5 and q % 2 == 1:
                tile_lo((q - 5) // 2)
        norm_quad(NQ - 1)
        tile_lo(len(ATT_TILES) - 2)
        tile_lo(len(ATT_TILES) - 1)
        for g in range(4):
            sc = gain[:, len(NORMS) * KD + g:len(NORMS) * KD + g + 1]
            dve.wait_ge(mix_hi_done, len(ATT_TILES) + g + 1)
            V.scalar_tensor_tensor(two(xn_lo[:, 4 + g, :]), slot(g % 2), sc,
                                   two(as32(xn_hi[:, 4 + g, :])), ALU.mult, ALU.subtract)\
                .then_inc(mix_ready, 1)
        b0 = STAGE["w_out"]
        for m in range(KD):
            dve.wait_ge(block_done, b0 + m + 1)
            V.tensor_tensor(two(h[:, m, :]), slot(m % 2), two(h[:, m, :]), ALU.add)\
                .then_inc(evac_done, 1)
            norm_lo(norm_of("ffn2_0"), m)
            split_lo_static(b0 + m + 2)
        ffn(1, "ffn2_0", norm_of("ffn1_1"), norm_of("ffn2_0"))
        ffn(2, "ffn1_1", norm_of("mix_1"), norm_of("ffn1_1"))

        nt = STAGE["tables"]
        variance(norm_of("mix_1"))
        split_lo_static(nt + 2)
        split_lo_static(nt + 3)
        cd = pd = 0
        for kind, g in CD_ORDER:
            if kind == "cd":
                for i, (t0, rows, s) in enumerate(FT_TILES):
                    dve.wait_ge(cd_hi, cd + 1)
                    V.scalar_tensor_tensor(y_lo[0:rows, g % 2, i, :], banks[0:rows, cd_bank(cd), 0:DCOL],
                                           rstd_tok[0:rows, i:i + 1], as32(y_hi[0:rows, g % 2, i, :]),
                                           ALU.mult, ALU.subtract).then_inc(cd_done, 1)
                    cd += 1
            elif kind == "pd":
                for part in range(2):
                    dve.wait_ge(pd_hi, pd + 1)
                    V.tensor_tensor(xn_lo[:, 2 * g + part, 0:NF], banks[:, 4 + pd % 4, 0:NF],
                                    as32(xn_hi[:, 2 * g + part, 0:NF]), ALU.subtract)\
                        .then_inc(pd_done, 1)
                    pd += 1
            else:
                dve.wait_ge(pd_hi, pd + 1)
                V.tensor_tensor(px_lo[0:MX, :], banks[0:MX, 4 + pd % 4, 0:NF],
                                as32(px_hi[0:MX, :]), ALU.subtract).then_inc(pd_done, 1)
        nf = STAGE["w_fourier"]
        split_lo_static(nf)
        split_lo_static(nf + 1)
        for m in range(KD):
            dve.wait_ge(odd_done, m + 1)
            s0, L = SEQS[1]
            half = L // 2 + 1
            fwd, bwd = h[:, m, s0:s0 + half], h[:, m, s0 + half:s0 + L]
            V.tensor_tensor(fwd, fwd, odd[:, FOLD[0]:FOLD[0] + half], ALU.add)
            V.tensor_tensor(bwd, bwd, odd[:, FOLD[0] + half - 2:FOLD[0]:-1], ALU.subtract)\
                .then_inc(odd_sample, 1)
            dve.wait_ge(odd_sample, m + 1)
            dve.wait_ge(odd_added, 2 * m + 2)
            even = banks[:, 2 * (m % 2), :]
            c0 = 0
            for s, (s0, L) in enumerate(SEQS):
                half = L // 2 + 1
                fwd = h[:, m, s0:s0 + half]
                bwd = h[:, m, s0 + half:s0 + L]
                V.tensor_tensor(fwd, even[:, c0:c0 + half], fwd, ALU.add)
                last = V.tensor_tensor(bwd, even[:, c0 + half - 2:c0:-1], bwd, ALU.add)
                c0 += FOLD[s]
            last.then_inc(evac_done, 1)
            norm_lo(norm_of("ffn2_1"), m)
            split_lo_static(nf + m + 2)
        ffn(3, "ffn2_1", norm_of("final"), norm_of("ffn2_1"))
        variance(norm_of("final"))
        spread(norm_of("final"))
        for m in range(KD):
            i = norm_of("final")
            V.scalar_tensor_tensor(h[:, m, :], h[:, m, :], gain[:, i * KD + m:i * KD + m + 1],
                                   rstd[:, :], ALU.mult, ALU.mult).then_inc(y_done, 1)

    @block.tensor
    def _(pe):
        M = nc.tensor

        def triple(out, lhs, rhs, first, last, opening=None):
            (a_hi, a_lo), (b_hi, b_lo) = lhs, rhs
            for j, (a, b) in enumerate(((a_hi, b_hi), (a_hi, b_lo), (a_lo, b_hi))):
                ins = M.matmul(out, a, b, start=first and j == 0, stop=last and j == 2)
                if opening and j == 0:
                    ins.then_inc(*opening)
            return ins

        def token_halves(s, lhs, rhs_hi, rhs_lo, cols, first, last):
            for j, (a, b) in enumerate(((lhs[0], rhs_hi), (lhs[0], rhs_lo), (lhs[1], rhs_hi))):
                for half in range(2):
                    ins = M.matmul(banks[:, 2 * s + half, 0:cols], a,
                                   b[:, half * cols:(half + 1) * cols],
                                   start=first and j == 0, stop=last and j == 2)
            return ins

        def open_block(s, n_half):
            pe.wait_ge(w_ready, n_half * 2 + (s + 1))
            if not (isinstance(n_half, int) and n_half == 0):
                pe.wait_ge(evac_done, n_half * 2 + (s - 1))

        def run_block(s, k, rhs, cols, before=None):
            for kt in range(k):
                if before:
                    before(kt)
                lhs = (w_hi[s][:, kt * P:(kt + 1) * P], w_lo[s][:, kt * P:(kt + 1) * P])
                ins = token_halves(s, lhs, *rhs(kt), cols, kt == 0, kt == k - 1)
            ins.then_inc(block_done, 1)

        def xn(kt):
            return xn_hi[:, kt, :], xn_lo[:, kt, :]

        def act_part(kt):
            return act_hi[:, kt * T:(kt + 1) * T], act_lo[:, kt * T:(kt + 1) * T]

        def statistics(i):
            pe.wait_ge(sum_done, 9 * i + 9)
            pe.wait_ge(setup_done, 2)
            tiles = [(100 * k, 100) for k in range(KD)]
            if i == norm_of("mix_1"):
                tiles = [(t0, rows) for t0, rows, _ in FT_TILES]
            for k, (t0, rows) in enumerate(tiles):
                ins = M.matmul(banks[0:rows, STAT, k:k + 1], sum_sq[:, t0:t0 + rows], ones[:, 0:1],
                               start=True, stop=True)
            ins.then_inc(stat_done, 1)

        def broadcast(i):
            pe.wait_ge(diag_done, BCAST_NORMS.index(i) + 1)
            halves = FFN_TOKENS[NORM_FFN.get(NORMS[i], 1)]
            for half, bank_runs in enumerate(halves):
                c = 0
                for t, n in bank_runs:
                    ins = M.matmul(banks[:, AUX + half, c:c + n], ones[0:100, :],
                                   diag[0:100, t:t + n], start=True, stop=True)
                    c += n
            ins.then_inc(bcast_done, 1)

        def first_blocks(n, i):
            cols = FFN_COLS[NORM_FFN[NORMS[i]]] if NORMS[i] in NORM_FFN else TH
            if i in LATE_NORMS:
                statistics(i)
                open_block(0, n // 2)
                open_block(1, n // 2)
                for kt in range(KD):
                    pe.wait_ge(xn_ready, i * KD + kt + 1)
                    if kt == 4:
                        broadcast(i)
                    for s in range(2):
                        lhs = (w_hi[s][:, kt * P:(kt + 1) * P], w_lo[s][:, kt * P:(kt + 1) * P])
                        ins = token_halves(s, lhs, *xn(kt), cols, kt == 0, kt == KD - 1)
                        if kt == KD - 1:
                            ins.then_inc(block_done, 1)
                return
            open_block(0, n // 2)
            run_block(0, KD, xn, cols, lambda kt: pe.wait_ge(xn_ready, i * KD + kt + 1))
            statistics(i)
            open_block(1, n // 2)
            run_block(1, KD, xn, cols, lambda kt: broadcast(i) if kt == 4 else None)

        def ffn(f, stage, norm_before):
            n0 = STAGE[stage]
            for half in range(2):
                b0 = n0 + half * (2 * HALF + KD)
                if half == 0:
                    first_blocks(b0, norm_before)
                with M.Fori(1 - half, HALF) as i:
                    for s in range(2):
                        open_block(s, i + b0 // 2)
                        run_block(s, KD, xn, FFN_COLS[f])
                d0 = b0 + 2 * HALF
                jj = f * FF_TILES + half * HALF
                pe.wait_ge(act_ready, jj + HALF - 1)
                with M.Fori(0, KD // 2) as i:
                    for s in range(2):
                        open_block(s, i + d0 // 2)
                        run_block(s, HALF, act_part, FFN_COLS[f], lambda kt: pe.wait_ge(act_ready, jj + HALF)
                                  if kt == HALF - 1 and s == 0 else None)

        def stage_blocks(stage, lo=0, count=KD, before=None):
            b0 = STAGE[stage]
            with M.Fori(lo // 2, count // 2) as i:
                for s in range(2):
                    open_block(s, i + b0 // 2)
                    run_block(s, KD, xn, TH)

        pe.wait_ge(const_in, 48)
        ffn(0, "ffn1_0", norm_of("ffn1_0"))

        b0 = STAGE["w_in"]
        first_blocks(b0, norm_of("mix_0"))
        stage_blocks("w_in", 2, N_IN)
        pe.wait_ge(evac_done, b0 + N_IN)
        for i, (s0, L, t, rows) in enumerate(ATT_TILES):
            if i >= 2:
                pe.wait_ge(v_tok_done, i - 1)
            M.transpose(banks[0:rows, 6 + i % 2, 0:P], v_sb[:, s0 + t:s0 + t + rows], ident[:, :])\
                .then_inc(v_tok_ps, 1)

        def scores(u):
            i, hd = UNITS[u]
            s0, L, t, rows = ATT_TILES[i]
            k0, k1 = keys_of(i)
            side = 64 * (hd // 4)
            if u >= 3:
                pe.wait_ge(score_done, u - 2)
            M.matmul(banks[0:rows, u % 3, 0:k1 - k0],
                     q_sb[side:side + 64, hd % 4, s0 + t:s0 + t + rows],
                     k_sb[side:side + 64, s0 + k0:s0 + k1], start=True, stop=True)\
                .then_inc(score_ps, 1)

        def transposes(u):
            i, hd = UNITS[u]
            rows = ATT_TILES[i][3]
            k0, k1 = keys_of(i)
            pe.wait_ge(norm_done, u + 1)
            if u >= 2:
                pe.wait_ge(prob_t_done, TCOUNT[u - 1])
            for j in range((k1 - k0 + P - 1) // P):
                kr = min(P, k1 - k0 - j * P)
                ins = M.transpose(banks[0:kr, 3 + u % 2, j * P:j * P + rows],
                                  score[0:rows, u % SCORES, j * P:j * P + kr],
                                  ident[0:rows, 0:rows])
            ins.then_inc(prob_t_ps, 1)

        def times_v(q):
            i = q // 2
            s0, L, t, rows = ATT_TILES[i]
            k0, k1 = keys_of(i)
            side = 64 * (q % 2)
            pe.wait_ge(prob_t_done, TCOUNT[4 * q + 4])
            if q == 0:
                pe.wait_ge(v_tok_done, len(ATT_TILES))
            if q % 2 == 0 and i >= 3:
                pe.wait_ge(mix_ready, i - 2)
            n = (k1 - k0 + P - 1) // P
            tile0 = i - t // P + k0 // P
            for j in range(n):
                kr = min(P, k1 - k0 - j * P)
                out = banks[side:side + 64, 5 + i % 3, :].rearrange("p (k r) -> p k r", k=4)
                ins = M.matmul(out[:, :, 0:rows], v_tok[0:kr, tile0 + j, side:side + 64],
                               prob_t[0:kr, q % 2, j, :, 0:rows], start=j == 0, stop=j == n - 1)
            ins.then_inc(quad_out, 1)

        TCOUNT = [0]
        for i, hd in UNITS:
            k0, k1 = keys_of(i)
            TCOUNT.append(TCOUNT[-1] + (2 if (k1 - k0) % P else 1))
        NU = len(UNITS)
        AHEAD = 8
        for u in range(NU + AHEAD):
            if u < NU:
                scores(u)
            v = u - AHEAD
            if v >= 0:
                transposes(v)
                if v % 4 == 1 and v > 4:
                    times_v(v // 4 - 1)
        times_v(NU // 4 - 1)
        for g in range(4):
            pe.wait_ge(pooled_done, g + 1)
            if g == 0:
                pe.wait_ge(mix_in, 48)
                pe.wait_ge(score_done, NU)
                pe.wait_ge(prob_t_done, TCOUNT[-1])
            if g >= 2:
                pe.wait_ge(mix_ready, len(ATT_TILES) + g - 1)
            cut = L_PROMPT - TH
            s = g % 2
            M.matmul(banks[:, 2 * s, 0:TH], pool_w[:, g, :], u_pad[:, g, PAD:PAD + TH],
                     start=True, stop=True)
            M.matmul(banks[:, 2 * s + 1, 0:cut], pool_w[:, g, :],
                     u_pad[:, g, PAD + TH:PAD + L_PROMPT], start=True, stop=True)
            M.matmul(banks[:, 2 * s + 1, cut:TH], pool_w[:, g, :],
                     u_pad[:, g, POOL_AT[1]:POOL_AT[1] + L_SAMPLE], start=True, stop=True)\
                .then_inc(pool_ps, 1)
        pe.wait_ge(mix_ready, len(ATT_TILES) + 4)
        stage_blocks("w_out")
        ffn(1, "ffn2_0", norm_of("ffn2_0"))
        ffn(2, "ffn1_1", norm_of("ffn1_1"))

        im = norm_of("mix_1")
        nt = STAGE["tables"]
        pe.wait_ge(w_ready, nt + 1)
        pe.wait_ge(evac_done, nt)
        cd = pd = 0
        for kind, g in CD_ORDER:
            if kind == "cd":
                for i, (t0, rows, s) in enumerate(FT_TILES):
                    if cd >= len(FIRST_CD):
                        pe.wait_ge(cd_done, cd - 3)
                    for kt in range(2):
                        if i == 0:
                            pe.wait_ge(xn_ready, im * KD + 2 * g + kt + 1)
                        x_pair = (xn_hi[:, 2 * g + kt, t0:t0 + rows], xn_lo[:, 2 * g + kt, t0:t0 + rows])
                        ins = triple(banks[0:rows, cd_bank(cd), 0:DCOL], x_pair,
                                     (dft_hi[:, kt, :], dft_lo[:, kt, :]), kt == 0, kt == 1,
                                     (block_done, N_TABLE) if cd == kt == 0 else None)
                    ins.then_inc(cd_ps, 1)
                    cd += 1
                    if cd == 3:
                        statistics(im)
            else:
                parts = range(2) if kind == "pd" else range(1)
                for part in parts:
                    if pd == 0:
                        pe.wait_ge(w_ready, nt + N_TABLE)
                    if pd >= 4:
                        pe.wait_ge(pd_done, pd - 3)
                    if kind == "pd":
                        pe.wait_ge(cd_done, 8 * (g + 1))
                    else:
                        pe.wait_ge(yx_done, 16)
                    c0 = 0
                    for s in range(2):
                        tiles = [i for i, x_ in enumerate(FT_TILES) if x_[2] == s]
                        rows = FT[s][0]
                        for i in tiles:
                            if kind == "pd":
                                a, b = y_hi[0:rows, g % 2, i, part * P:(part + 1) * P], \
                                    y_lo[0:rows, g % 2, i, part * P:(part + 1) * P]
                                out = banks[:, 4 + pd % 4, c0:c0 + FOLD[s]]
                            else:
                                a, b = yx_hi[0:rows, i, :], yx_lo[0:rows, i, :]
                                out = banks[0:MX, 4 + pd % 4, c0:c0 + FOLD[s]]
                            at = cs_at(i, part)
                            ins = triple(out, (a, b), (cs_hi[0:rows, at:at + FOLD[s]],
                                                       cs_lo[0:rows, at:at + FOLD[s]]),
                                         i == tiles[0], i == tiles[-1])
                        c0 += FOLD[s]
                    ins.then_inc(pd_ps, 1)
                    pd += 1
        nf = STAGE["w_fourier"]
        pe.wait_ge(pd_done, pd)
        for m in range(KD):
            n = nf + m
            open_block(n % 2, n // 2)
            s = n % 2
            even, odd_ps = banks[:, 2 * s, 0:NF], banks[:, 2 * s + 1, 0:NF]
            for g in range(4):
                lhs = [w[s][:, g * P:(g + 1) * P] for w in (w_hi, w_lo)]
                triple(even, lhs, (xn_hi[:, 2 * g, 0:NF], xn_lo[:, 2 * g, 0:NF]), g == 0, False)
            lhs = [w[s][0:MX, 8 * P:9 * P] for w in (w_hi, w_lo)]
            triple(even, lhs, (px_hi[0:MX, :], px_lo[0:MX, :]), False, True)
            for g in range(4):
                lhs = [w[s][:, (4 + g) * P:(5 + g) * P] for w in (w_hi, w_lo)]
                ins = triple(odd_ps, lhs, (xn_hi[:, 2 * g + 1, 0:NF], xn_lo[:, 2 * g + 1, 0:NF]),
                             g == 0, g == 3)
            ins.then_inc(block_done, 1)
        ffn(3, "ffn2_1", norm_of("ffn2_1"))
        statistics(norm_of("final"))
        broadcast(norm_of("final"))

    ctx.close()


def alibi_table():
    r = np.arange(P)[:, None]
    j = np.arange(KEYS)[None, :] - P
    dist = np.abs(j - r)
    slopes = np.exp2(-8.0 * np.arange(1, N_HEADS + 1) / N_HEADS)
    table = np.where(dist[:, None, :] <= WINDOW, -slopes[None, :, None] * dist[:, None, :], NEG_INF)
    return table.astype(np.float32).reshape(P, N_HEADS * KEYS)


def edge_table():
    out = np.ones((4, 2, 2, PAD))
    for g, w in enumerate(POOL_WINDOWS):
        for s, (_, L) in enumerate(SEQS):
            t = np.arange(L)
            count = np.clip(t + w - w // 2, 0, L) - np.clip(t - w // 2, 0, L)
            out[g, s, 0], out[g, s, 1] = w / count[:PAD], w / count[-PAD:]
    return np.ascontiguousarray(np.broadcast_to(out.astype(np.float32).reshape(1, -1), (P, 4 * 4 * PAD)))


def dft_tables():
    out = np.zeros((N_TABLE, P, KMAX * P))
    n = np.arange(GROUP)[:, None]
    k = np.arange(P)[None, :]
    d = np.zeros((GROUP, DCOL))
    d[:, 0:P] = np.cos(2 * np.pi * (n * k % GROUP) / GROUP)
    d[:, P + 1:GROUP] = np.sin(2 * np.pi * (n * k[:, 1:] % GROUP) / GROUP)
    d[:, GROUP] = np.cos(np.pi * n[:, 0])
    out[0, :, 0:2 * DCOL] = d.reshape(2, P, DCOL).transpose(1, 0, 2).reshape(P, 2 * DCOL)
    cols = []
    for s, (rows, starts) in enumerate(FT):
        L = SEQS[s][1]
        norm = 1.0 / np.sqrt(GROUP * L)
        done = 0
        for t0 in starts:
            t = t0 + np.arange(rows)[:, None]
            angle = 2 * np.pi * ((t * np.arange(FOLD[s])[None, :]) % L) / L
            own = t >= done
            done = t0 + rows
            for f in (np.cos(angle), np.sin(angle)):
                f = np.where(own, f * norm, 0.0)
                f[np.abs(f) < 1e-14] = 0.0
                full = np.zeros((P, FOLD[s]))
                full[:rows] = f
                cols.append(full)
    cs = np.concatenate(cols, axis=1)
    for r, (a, b) in enumerate(((0, 4 * FOLD[0]), (4 * FOLD[0], 8 * FOLD[0]), (8 * FOLD[0], cs.shape[1]))):
        out[1 + r, :, 0:b - a] = cs[:, a:b]
    return out.astype(np.float32)


def kernel(**inputs):
    import concourse.bacc as bacc
    from concourse.bass_utils import run_bass_kernel_spmd

    a = {k: np.asarray(v) for k, v in inputs.items()}

    def columns(w, kt):
        lead = w.shape[:-2]
        w = w.reshape(*lead, kt, P, w.shape[-1] // P, P)
        n = len(lead)
        w = w.transpose(*range(n), n + 2, n + 1, n, n + 3)
        return w.reshape(*lead, w.shape[n], P, kt * P)

    tokens = np.concatenate([a["meta_tokens"], a["x_prompt"][0], a["meta_tokens"], a["x_sample"][0]])
    x = tokens.T.reshape(KD, P, T).transpose(1, 0, 2).reshape(P, KD * T)
    norms = [a["norm_ffn1"][0], a["norm_mix"][0], a["norm_ffn2"][0], a["norm_ffn1"][1],
             a["norm_mix"][1], a["norm_ffn2"][1], a["norm_final"], a["pool_scale"][0]]
    gains = np.concatenate(norms).reshape(-1, P).T
    sinks = np.broadcast_to(a["attn_sink"][0][None, :], (P, N_HEADS))
    gate_up, down = [], []
    for layer in range(2):
        for f in (1, 2):
            g = columns(a[f"ffn{f}_w_gate"][layer], KD)
            u = columns(a[f"ffn{f}_w_up"][layer], KD)
            gate_up.append(np.stack([g, u], axis=1).reshape(2 * FF_TILES, P, KD * P))
            down.append(columns(a[f"ffn{f}_w_down"][layer].reshape(2, HALF * P, D_MODEL), HALF)
                        .reshape(2 * KD, P, HALF * P))
    w = a["w_in_ap"][0]
    q = w[:, 0:512].reshape(D_MODEL, 2, 4, HEAD_DIM).transpose(0, 2, 1, 3).reshape(D_MODEL, 512)
    w_in = columns(np.concatenate([w[:, 768:], w[:, 640:768], w[:, 512:640], q], axis=1), KD)
    wo = a["w_out_ap"][0]
    heads = wo[:512].reshape(2, 4, HEAD_DIM, D_MODEL).transpose(1, 0, 2, 3).reshape(512, D_MODEL)
    w_out = columns(np.concatenate([heads, wo[512:]]), KD)
    pool_w = a["pool_w"][0].transpose(1, 0, 2).reshape(P, 4 * P)
    wf = a["w_out_fourier"][0].reshape(4, GROUP, D_MODEL)
    low = wf[:, 0:P]
    high = np.concatenate([np.zeros((4, 1, D_MODEL), wf.dtype), wf[:, :P:-1]], axis=1)
    mid = np.concatenate([wf[:, P], np.zeros((P - 4, D_MODEL), wf.dtype)])
    w_fourier = columns(np.concatenate([low.reshape(4 * P, -1), high.reshape(4 * P, -1), mid]), FK)

    arrays = {
        "x": x, "gains": gains, "sinks": sinks, "ident_in": np.eye(P, dtype=np.float32),
        "alibi_in": alibi_table(), "edges_in": edge_table(), "pool_w_in": pool_w,
        "tables": dft_tables(), "gate_up": np.stack(gate_up), "down": np.stack(down), "w_in": w_in,
        "w_out": w_out, "w_fourier": w_fourier,
    }
    nc = bacc.Bacc("TRN2", target_bir_lowering=False, num_devices=1)
    launched, args = {}, []
    for name, value in arrays.items():
        value = np.ascontiguousarray(value)
        launched[name + "_dram"] = value
        args.append(nc.dram_tensor(name + "_dram", value.shape, mybir.dt.from_np(value.dtype),
                                   kind="ExternalInput").ap())
    args.append(nc.dram_tensor("y_dram", (P, KD * T), mybir.dt.float32, kind="ExternalOutput").ap())
    build(nc, *args)
    r = run_bass_kernel_spmd(nc, [launched], core_ids=[0])
    y = r.results[0]["y_dram"].reshape(P, KD, T).transpose(2, 1, 0).reshape(T, D_MODEL)
    return (np.ascontiguousarray(y[N_META:L_PROMPT])[None],
            np.ascontiguousarray(y[L_PROMPT + N_META:])[None])
```
